# Optimizing a Trainium2 kernel written in Bass

```python
import math
import jax, jax.numpy as jnp
from jax import lax
import numpy as np

D_MODEL = 1024
BATCH = 1
SEQ = 256
DEPTH = 2

A_CH = 512
CONV_W = 31
B_HEADS = 8
B_HEAD_DIM = 64
B_CH = B_HEADS * B_HEAD_DIM
SGU_CHUNK = 128
MIX_IN = 2 * A_CH + 2 * B_CH
MIX_OUT = A_CH + B_CH
MOBA_HEADS = 16
MOBA_HEAD_DIM = 64
MOBA_BLOCK = 256
MOBA_TOPK = 3
MOBA_Q_BLOCK = 128
REL_BUCKETS = 32
REL_MAX_DIST = 2048
PEER_HEADS = 8
PEER_NKEYS = 128
PEER_N_EXPERTS = PEER_NKEYS * PEER_NKEYS
PEER_DKEY = 256
PEER_TOPK = 16
PEER_TOKEN_BLOCK = 128
EPS = 1e-6
NEG = -1e30

kernel_name = "hybrid_conv_sgu_moba_peer"

def rms_norm(x, g):
    xf = x.astype(jnp.float32)
    y = xf * lax.rsqrt(jnp.mean(xf * xf, axis=-1, keepdims=True) + EPS)
    return (y * g.astype(jnp.float32)).astype(x.dtype)

def layer_norm(x, g, b):
    xf = x.astype(jnp.float32)
    mu = jnp.mean(xf, axis=-1, keepdims=True)
    var = jnp.mean(jnp.square(xf - mu), axis=-1, keepdims=True)
    y = (xf - mu) * lax.rsqrt(var + EPS)
    return (y * g.astype(jnp.float32) + b.astype(jnp.float32)).astype(x.dtype)

def t5_bucket(dist):
    n = jnp.maximum(dist, 0)
    max_exact = REL_BUCKETS // 2
    nf = jnp.maximum(n, 1).astype(jnp.float32)
    log_b = max_exact + (jnp.log(nf / max_exact) / math.log(REL_MAX_DIST / max_exact)
                         * (REL_BUCKETS - max_exact)).astype(jnp.int32)
    return jnp.where(n < max_exact, n, jnp.minimum(log_b, REL_BUCKETS - 1))

def conv_sgu_mixer(h, w_in, conv_w, conv_b, conv_ln_g, conv_ln_b,
                   sgu_ln_g, sgu_ln_b, sgu_w, sgu_b, w_out):
    B, S, _ = h.shape
    z = h @ w_in
    a_val, a_gate, b_u, b_v = jnp.split(z, [A_CH, 2 * A_CH, 2 * A_CH + B_CH], axis=-1)
    a = a_val * jax.nn.sigmoid(a_gate)
    a = lax.conv_general_dilated(
        a, conv_w.reshape(CONV_W, 1, A_CH), window_strides=(1,),
        padding=[(CONV_W - 1, 0)], dimension_numbers=('NWC', 'WIO', 'NWC'),
        feature_group_count=A_CH) + conv_b
    a = jax.nn.silu(layer_norm(a, conv_ln_g, conv_ln_b))
    u = jax.nn.gelu(b_u)
    v = layer_norm(jax.nn.gelu(b_v), sgu_ln_g, sgu_ln_b)
    n_chunk = S // SGU_CHUNK
    v = v.reshape(B, n_chunk, SGU_CHUNK, B_HEADS, B_HEAD_DIM)
    mask = jnp.tril(jnp.ones((SGU_CHUNK, SGU_CHUNK), dtype=sgu_w.dtype))
    s = jnp.einsum('hts,bnshc->bnthc', sgu_w * mask, v) + sgu_b.T[None, None, :, :, None]
    bo = u * s.reshape(B, S, B_CH)
    return jnp.concatenate([a, bo], axis=-1) @ w_out

def moba_attention(q, k, v, rel_bias):
    B, S, H, hd = q.shape
    n_blk = -(-S // MOBA_BLOCK)
    s_pad = n_blk * MOBA_BLOCK
    pad = ((0, 0), (0, s_pad - S), (0, 0), (0, 0))
    kb = jnp.pad(k, pad).reshape(B, n_blk, MOBA_BLOCK, H, hd).transpose(0, 3, 1, 2, 4)
    vb = jnp.pad(v, pad).reshape(B, n_blk, MOBA_BLOCK, H, hd).transpose(0, 3, 1, 2, 4)
    k_mean = jnp.mean(kb.astype(jnp.float32), axis=3)
    gate = jnp.einsum('bshd,bhnd->bshn', q.astype(jnp.float32), k_mean)
    own_blk = jnp.arange(S) // MOBA_BLOCK
    past = jnp.arange(n_blk)[None, :] < own_blk[:, None]
    gate = jnp.where(past[None, :, None, :], gate, -jnp.inf)
    k_sel = min(MOBA_TOPK, n_blk)
    _, sel = lax.top_k(gate, k_sel)
    nqc = S // MOBA_Q_BLOCK
    qc_all = q.reshape(B * nqc, MOBA_Q_BLOCK, H, hd)
    sel_all = sel.reshape(B * nqc, MOBA_Q_BLOCK, H, k_sel)
    idx = jnp.arange(B * nqc)
    b_all = idx // nqc
    c_all = idx % nqc
    h_idx = jnp.arange(H)[None, :, None]
    offs = jnp.arange(MOBA_BLOCK)
    scale = hd ** -0.5
    n_past = k_sel * MOBA_BLOCK

    def step(args):
        qc, selc, b, c = args
        t = c * MOBA_Q_BLOCK + jnp.arange(MOBA_Q_BLOCK)
        own = (c * MOBA_Q_BLOCK) // MOBA_BLOCK
        kp = kb[b, h_idx, selc]
        vp = vb[b, h_idx, selc]
        ko = kb[b, :, own]
        vo = vb[b, :, own]
        dist_p = t[:, None, None, None] - (selc[..., None] * MOBA_BLOCK + offs)
        bias_p = rel_bias[t5_bucket(dist_p), h_idx[..., None]].astype(jnp.float32)
        lp = jnp.einsum('qhd,qhjkd->qhjk', qc, kp).astype(jnp.float32) * scale + bias_p
        lp = jnp.where((selc < own)[..., None], lp, NEG)
        dist_o = t[:, None] - (own * MOBA_BLOCK + offs)
        bias_o = rel_bias[t5_bucket(dist_o)].transpose(0, 2, 1).astype(jnp.float32)
        lo = jnp.einsum('qhd,hkd->qhk', qc, ko).astype(jnp.float32) * scale + bias_o
        lo = jnp.where((dist_o >= 0)[:, None, :], lo, NEG)
        logits = jnp.concatenate([lp.reshape(MOBA_Q_BLOCK, H, n_past), lo], axis=-1)
        p = jax.nn.softmax(logits, axis=-1).astype(vb.dtype)
        pp = p[..., :n_past].reshape(MOBA_Q_BLOCK, H, k_sel, MOBA_BLOCK)
        po = p[..., n_past:]
        return (jnp.einsum('qhjk,qhjkd->qhd', pp, vp)
                + jnp.einsum('qhk,hkd->qhd', po, vo))

    out = lax.map(step, (qc_all, sel_all, b_all, c_all))
    return out.reshape(B, S, H * hd)

def moba_mixer(h, w_qkv, w_o, rel_bias):
    B, S, _ = h.shape
    qkv = (h @ w_qkv).reshape(B, S, 3, MOBA_HEADS, MOBA_HEAD_DIM)
    o = moba_attention(qkv[:, :, 0], qkv[:, :, 1], qkv[:, :, 2], rel_bias)
    return o @ w_o

def peer(h, w_q, subkeys, u_tab, v_tab):
    B, S, D = h.shape
    T = B * S
    xt = h.reshape(T, D)
    q = (xt @ w_q).reshape(T, PEER_HEADS, 2, PEER_DKEY // 2)
    s = jnp.einsum('thpd,hpkd->thpk', q, subkeys).astype(jnp.float32)
    s1, i1 = lax.top_k(s[:, :, 0], PEER_TOPK)
    s2, i2 = lax.top_k(s[:, :, 1], PEER_TOPK)
    cand = (s1[..., :, None] + s2[..., None, :]).reshape(T, PEER_HEADS, PEER_TOPK * PEER_TOPK)
    sc, ci = lax.top_k(cand, PEER_TOPK)
    ei = jnp.take_along_axis(i1, ci // PEER_TOPK, axis=-1)
    ej = jnp.take_along_axis(i2, ci % PEER_TOPK, axis=-1)
    expert = ei * PEER_NKEYS + ej
    g = jax.nn.softmax(sc, axis=-1).astype(h.dtype)
    nc = T // PEER_TOKEN_BLOCK

    def step(args):
        xc, ec, gc = args
        uc = u_tab[ec]
        vc = v_tab[ec]
        act = jax.nn.gelu(jnp.einsum('td,thkd->thk', xc, uc))
        return jnp.einsum('thk,thkd->td', gc * act, vc)

    y = lax.map(step, (xt.reshape(nc, PEER_TOKEN_BLOCK, D),
                       expert.reshape(nc, PEER_TOKEN_BLOCK, PEER_HEADS, PEER_TOPK),
                       g.reshape(nc, PEER_TOKEN_BLOCK, PEER_HEADS, PEER_TOPK)))
    return y.reshape(B, S, D)

def setup_inputs(seed: int = 0) -> dict:
    key = jax.random.key(seed)
    ks = jax.random.split(key, 24)
    n_even = (DEPTH + 1) // 2
    n_odd = DEPTH // 2
    f32 = jnp.float32

    def nrm(k, shape, scale):
        return jax.random.normal(k, shape, f32) * scale

    attn_w = MOBA_HEADS * MOBA_HEAD_DIM
    return {
        "x": nrm(ks[0], (BATCH, SEQ, D_MODEL), 1.0),
        "ev_w_in": nrm(ks[1], (n_even, D_MODEL, MIX_IN), D_MODEL ** -0.5),
        "ev_conv_w": nrm(ks[2], (n_even, CONV_W, A_CH), CONV_W ** -0.5),
        "ev_conv_b": nrm(ks[3], (n_even, A_CH), 0.02),
        "ev_conv_ln_g": 1.0 + nrm(ks[4], (n_even, A_CH), 0.02),
        "ev_conv_ln_b": nrm(ks[5], (n_even, A_CH), 0.02),
        "ev_sgu_ln_g": 1.0 + nrm(ks[6], (n_even, B_CH), 0.02),
        "ev_sgu_ln_b": nrm(ks[7], (n_even, B_CH), 0.02),
        "ev_sgu_w": nrm(ks[8], (n_even, B_HEADS, SGU_CHUNK, SGU_CHUNK), SGU_CHUNK ** -0.5),
        "ev_sgu_b": 1.0 + nrm(ks[9], (n_even, B_HEADS, SGU_CHUNK), 0.02),
        "ev_w_out": nrm(ks[10], (n_even, MIX_OUT, D_MODEL), MIX_OUT ** -0.5),
        "od_w_qkv": nrm(ks[11], (n_odd, D_MODEL, 3 * attn_w), D_MODEL ** -0.5),
        "od_w_o": nrm(ks[12], (n_odd, attn_w, D_MODEL), attn_w ** -0.5),
        "rel_bias": nrm(ks[13], (REL_BUCKETS, MOBA_HEADS), 0.5),
        "peer_w_q": nrm(ks[14], (DEPTH, D_MODEL, PEER_HEADS * PEER_DKEY), D_MODEL ** -0.5),
        "peer_subkeys": nrm(ks[15], (DEPTH, PEER_HEADS, 2, PEER_NKEYS, PEER_DKEY // 2),
                            (PEER_DKEY // 2) ** -0.5),
        "peer_u": nrm(ks[16], (DEPTH, PEER_N_EXPERTS, D_MODEL), D_MODEL ** -0.5),
        "peer_v": nrm(ks[17], (DEPTH, PEER_N_EXPERTS, D_MODEL), PEER_HEADS ** -0.5),
        "norm_mix_g": 1.0 + nrm(ks[18], (DEPTH, D_MODEL), 0.02),
        "norm_ffn_g": 1.0 + nrm(ks[19], (DEPTH, D_MODEL), 0.02),
        "norm_final_g": 1.0 + nrm(ks[20], (D_MODEL,), 0.02),
    }

def reference(x, ev_w_in, ev_conv_w, ev_conv_b, ev_conv_ln_g, ev_conv_ln_b,
              ev_sgu_ln_g, ev_sgu_ln_b, ev_sgu_w, ev_sgu_b, ev_w_out,
              od_w_qkv, od_w_o, rel_bias, peer_w_q, peer_subkeys, peer_u, peer_v,
              norm_mix_g, norm_ffn_g, norm_final_g):
    for l in range(DEPTH):
        h = rms_norm(x, norm_mix_g[l])
        i = l // 2
        if l % 2 == 0:
            mix = conv_sgu_mixer(h, ev_w_in[i], ev_conv_w[i], ev_conv_b[i],
                                 ev_conv_ln_g[i], ev_conv_ln_b[i], ev_sgu_ln_g[i],
                                 ev_sgu_ln_b[i], ev_sgu_w[i], ev_sgu_b[i], ev_w_out[i])
        else:
            mix = moba_mixer(h, od_w_qkv[i], od_w_o[i], rel_bias)
        x = x + mix
        h = rms_norm(x, norm_ffn_g[l])
        x = x + peer(h, peer_w_q[l], peer_subkeys[l], peer_u[l], peer_v[l])
    return rms_norm(x, norm_final_g)


_drawn_inputs = setup_inputs


def setup_inputs(seed=0):
    import zlib

    import numpy as np

    out = dict(_drawn_inputs(seed))
    spreads = {}
    factors = {}
    for name, (base, spread) in spreads.items():
        noise = np.random.default_rng([zlib.crc32(name.encode()), seed]).standard_normal(out[name].shape)
        drawn = base * np.exp(spread * noise) if base else spread * noise
        out[name] = __import__('jax').numpy.asarray(drawn.astype(out[name].dtype))
    for name, factor in factors.items():
        out[name] = (out[name] * factor).astype(out[name].dtype)
    return out
```

```python
import math
from contextlib import ExitStack

import concourse.bass as bass
import numpy as np
from concourse import mybir

F32 = mybir.dt.float32
F32R = mybir.dt.float32r
I32 = mybir.dt.int32
U32 = mybir.dt.uint32
ALU = mybir.AluOpType
ACT = mybir.ActivationFunctionType
AX = mybir.AxisListType.X

P = 128
T = 256
TT = T // P
D = 1024
KD = D // P
HALF = D // 2
CONV = 31
CH = 512
KC = CH // P
SGU_HEADS = 8
HEADS = 16
HD = 64
NKEYS = 128
PEER_HEADS = 8
TOPK = 16
UNITS = TT * PEER_HEADS
EPS = 1e-6
NEG = -1e30
LOWEST = -3.0e38
REL_BUCKETS = 32
REL_SPAN = 512
ROWS = [TOPK // (i + 1) for i in range(TOPK)]
ROW_AT = [sum(ROWS[:i]) for i in range(TOPK)]
CANDS = sum(ROWS)
ROW_GROUPS = [(0, 1, 16), (1, 1, 8), (2, 1, 5), (3, 1, 4), (4, 1, 3), (5, 3, 2), (8, 8, 1)]

STREAM = [("w_in", 16, True), ("w_out", 8, True), ("q0", 16, True), ("u0", NKEYS, True), ("v0", NKEYS, False),
          ("qkv", 24, True), ("w_o", 8, True), ("q1", 16, True), ("u1", NKEYS, True), ("v1", NKEYS, False)]
TILE0, PROJ0 = {}, {}
_n = _p = 0
for _name, _tiles, _proj in STREAM:
    TILE0[_name], PROJ0[_name] = _n, _p
    _n += _tiles
    _p += _tiles if _proj else 0
TILES = _n
PARAMS = 8
RAW = 4
SPLIT = 4

PICK_TURNS = UNITS // 2 + 1


def bucket_of_distance():
    exact, span = REL_BUCKETS // 2, 2048
    out = []
    for n in range(T):
        if n < exact:
            out.append(n)
        else:
            f = np.float32(np.log(np.float32(n) / np.float32(exact))) / np.float32(math.log(span / exact))
            out.append(min(exact + int(np.float32(f * np.float32(REL_BUCKETS - exact))), REL_BUCKETS - 1))
    return out


def constants():
    c = np.zeros((P, 4 * P), np.float32)
    c[:, 0:P] = np.eye(P)
    c[:, P:2 * P] = np.eye(P)[::-1]
    c[:, 2 * P:3 * P] = 1.0
    c[:, 3 * P:4 * P] = np.arange(P)
    line = np.zeros((REL_BUCKETS + 1, REL_SPAN), np.float32)
    buckets = bucket_of_distance()
    for x in range(REL_SPAN):
        line[buckets[T - 1 - x] if x < T else REL_BUCKETS, x] = 1.0
    return c, line


def at_least(eng, sem, value):
    if not isinstance(value, int) or value > 0:
        eng.wait_ge(sem, value)


def sweep(eng, turns, body, first=0, last=0):
    for k in range(first):
        body(k)
    if turns - last > first:
        with eng.Fori(first, turns - last) as k:
            body(k)
    for k in range(turns - last, turns):
        body(k)


def build(nc, a, out):
    ctx = ExitStack()
    with ctx:
        def sb(name, shape, dt=F32):
            return ctx.enter_context(nc.sbuf_tensor(name, shape, dt))

        def sem(name):
            return ctx.enter_context(nc.semaphore(name))

        big = sb("big", [P, NKEYS * T])
        xT = sb("xT", [P, KD, T])
        x_hi = sb("x_hi", [P, KD, T], F32R)
        x_lo = sb("x_lo", [P, KD, T], F32R)
        raw = sb("raw", [P, RAW, D])
        w_hi = sb("w_hi", [P, SPLIT, HALF], F32R)
        w_lo = sb("w_lo", [P, SPLIT, HALF], F32R)
        picks = sb("picks", [P, 3, T])
        hot_j = sb("hot_j", [P, 8, P])
        hot_i = sb("hot_i", [P, 8, P])
        ag_hi = sb("ag_hi", [P, 2, T], F32R)
        ag_lo = sb("ag_lo", [P, 2, T], F32R)
        const = sb("const", [P, 4 * P])
        gains = sb("gains", [P, 5, KD])
        small = sb("small", [P, 6, KC])
        rstd = sb("rstd", [P, T])
        ident, anti, ones, iota = (const[:, P * i:P * (i + 1)] for i in range(4))

        psum = ctx.enter_context(nc.psum_tensor("psum", [P, 8, 512], F32))
        y_ps = psum[:, 0:4, :].rearrange("p b (m t) -> p (b m) t", t=T)
        proj_ps = [psum[:, 4 + i, 0:T] for i in range(2)]
        misc_ps = [psum[:, 6 + i, :] for i in range(2)]

        def room(at, *shape):
            n = math.prod(shape)
            v = big[:, at:at + n]
            if len(shape) == 2:
                v = v.rearrange("p (a b) -> p a b", b=shape[1])
            if len(shape) == 3:
                v = v.rearrange("p (a b c) -> p a b c", b=shape[1], c=shape[2])
            if len(shape) == 4:
                v = v.rearrange("p (a b c d) -> p a b c d", b=shape[1], c=shape[2], d=shape[3])
            return v, at + n

        top = NKEYS * T
        hT, _ = room(top - KD * T, KD, T)
        sq, _ = room(top - 2 * KD * T, KD, T)
        ms, _ = room(top - 2 * KD * T - 2 * T, 2, T)
        z0, at = room(0, 4, KC, T)
        sig, at = room(at, KC, T)
        guv, at = room(at, 2, KC, T)
        pad, at = room(at, KC, 288)
        conv, at = room(at, KC, T)
        centred, at = room(at, 2, KC, T)
        lnsq, at = room(at, 2, KC, T)
        lnstat, at = room(at, 2, 4, T)
        vn, at = room(at, KC, T)
        vT, at = room(at, TT, CH)
        sgu_w, at = room(at, SGU_HEADS, P)
        sgu_wm, at = room(at, SGU_HEADS, P)
        sgu_b, at = room(at, SGU_HEADS, P)
        conv_w, at = room(at, KC, CONV)
        rel, at = room(at, 1, HEADS)
        line, at = room(at, 1, REL_SPAN)
        bias_line, at = room(at, 1, REL_SPAN)
        z1, at = room(0, 24, T)
        v1T, at = room(at, TT, D)
        hankel, at = room(at, HEADS, 384)
        q_st, at = room(at, 2, T)
        k_st, at = room(at, 2, T)
        v_st, at = room(at, 2, TT, P)
        expd, at = room(at, 2, TT, T)
        prob, at = room(at, 2, TT, T)
        probT, at = room(at, 2, 3, P)
        soft, at = room(at, 2, 4, TT)
        subk, at = room(0, 2 * PEER_HEADS, P)
        qs, at = room(at, 2, T)
        at = 64 * T
        topv, at = room(at, UNITS, 2, TOPK)
        topi, at = room(at, UNITS, 2, TOPK)
        st_v, at = room(at, TT, TOPK)
        st_i, at = room(at, TT, TOPK)
        st_w, at = room(at, TT, P)
        st_s, at = room(at, TT, P)
        cand, at = room(at, UNITS, CANDS)
        cid, at = room(at, UNITS, CANDS)
        cst, at = room(at, 2, CANDS)
        cwk, at = room(at, 2, CANDS)
        pv, at = room(at, 2, TOPK)
        pi, at = room(at, 2, TOPK)
        pf, at = room(at, 2, TOPK)
        eq, at = room(at, 2, TOPK, CANDS)
        tv, at = room(at, UNITS, TOPK)
        ids, at = room(at, UNITS, TOPK)
        id_i, at = room(at, 3, UNITS * TOPK)
        id_f, at = room(at, 2, UNITS, TOPK)
        gsum, at = room(at, 2, UNITS)
        assert at <= top - 2 * KD * T

        loaded = [sem(f"loaded{i}") for i in range(RAW)]
        hi_ready = sem("hi_ready")
        split_ready = sem("split_ready")
        half_used = sem("half_used")
        proj_taken = sem("proj_taken")
        params_in = sem("params_in")
        x_in = sem("x_in")
        subk_in = sem("subk_in")
        hankel_in = sem("hankel_in")
        line_out = sem("line_out")
        out_done = sem("out_done")
        sq_ready = [sem(f"sq_ready{i}") for i in range(5)]
        ss_ready = [sem(f"ss_ready{i}") for i in range(5)]
        rstd_step = [sem(f"rstd_step{i}") for i in range(5)]
        rstd_ready = [sem(f"rstd_ready{i}") for i in range(5)]
        h_ready = [sem(f"h_ready{i}") for i in range(7)]
        x_hi_ready = [sem(f"x_hi_ready{i}") for i in range(6)]
        operand_ready = [sem(f"operand_ready{i}") for i in range(6)]
        line_ps = sem("line_ps")
        line_sb = sem("line_sb")
        neg_row = sem("neg_row")
        gated = sem("gated")
        pad_zero = sem("pad_zero")
        pad_ready = sem("pad_ready")
        conv_step = sem("conv_step")
        ln_step = [sem(f"ln_step{i}") for i in range(2)]
        ln_sum = [sem(f"ln_sum{i}") for i in range(2)]
        ln_root = [sem(f"ln_root{i}") for i in range(2)]
        silu_done = sem("silu_done")
        vn_ready = sem("vn_ready")
        vT_ps = sem("vT_ps")
        vT_ready = sem("vT_ready")
        masked = sem("masked")
        mixed = sem("mixed")
        x_added = sem("x_added")
        keys_scored = sem("keys_scored")
        rank_step = sem("rank_step")
        ranked = sem("ranked")
        scores_copied = sem("scores_copied")
        pick_step = sem("pick_step")
        build_step = sem("build_step")
        soft_in = sem("soft_in")
        soft_exp = sem("soft_exp")
        picks_ps = sem("picks_ps")
        picks_ready = sem("picks_ready")
        hot_ready = sem("hot_ready")
        scattered = sem("scattered")
        act_gated = sem("act_gated")
        ag_hi_ready = sem("ag_hi_ready")
        ag_ready = sem("ag_ready")
        y_added = sem("y_added")
        staged = sem("staged")
        v1T_ps = sem("v1T_ps")
        v1T_ready = sem("v1T_ready")
        scores_ready = sem("scores_ready")
        soft_step = sem("soft_step")
        exp_ready = sem("exp_ready")
        prob_ready = sem("prob_ready")
        probT_ps = sem("probT_ps")
        probT_ready = sem("probT_ready")
        heads_out = sem("heads_out")
        pair_taken = sem("pair_taken")

        SRC = dict(zip([n for n, _, _ in STREAM], [a["w_in"], a["w_out"], a["peer_q"][0], a["peer_u"][0], a["peer_v"][0],
                                                    a["w_qkv"], a["w_o"], a["peer_q"][1], a["peer_u"][1], a["peer_v"][1]]))
        scratch = nc.dram_tensor("bias_scratch", (HEADS, REL_SPAN), F32)
        scratch_ap = scratch.ap()

        def loaded_count(name, k, j):
            return 16 * (TILE0[name] // RAW + k + j // RAW + 1)

        block = ctx.enter_context(nc.Block())

        @block.sync
        def _(sp):
            sp.dma_start(xT[:], a["xT"].rearrange("(k p) t -> p k t", p=P)).then_inc(x_in, 16)

            def load(name, src, k):
                for j in range(RAW):
                    at_least(sp, split_ready, 2 * (TILE0[name] + 4 * k + j - RAW) + 2)
                    sp.dma_start(raw[:, j, :], src[4 * k + j]).then_inc(loaded[j], 16)

            for name, tiles, _ in STREAM:
                sweep(sp, tiles // RAW, lambda k: load(name, SRC[name], k), first=1 if name == "w_in" else 0)
            o = out.rearrange("(k p) t -> p k t", p=P)
            for g in range(4):
                sp.wait_ge(h_ready[6], 2 * g + 2)
                sp.dma_start(o[:, 2 * g:2 * g + 2, :], hT[:, 2 * g:2 * g + 2, :]).then_inc(out_done, 16)
            sp.wait_ge(out_done, 64)

        @block.gpsimd
        def _(pool):
            for dst, src in ((const[:], a["const"]), (gains[:], a["gains"]), (small[:, 0:5, :], a["small"]),
                             (conv_w, a["conv_w"]), (rel[0:REL_BUCKETS, 0, :], a["rel"]),
                             (line[0:REL_BUCKETS + 1, 0, :], a["line"]),
                             (sgu_w, a["sgu_w"])):
                pool.dma_start(dst, src).then_inc(params_in, 16)
            pool.dma_start(sgu_b[0:1], a["sgu_b"]).then_inc(params_in, 16)
            pool.memset(rel[REL_BUCKETS:REL_BUCKETS + 1, 0, :], NEG).then_inc(neg_row, 1)
            pool.wait_ge(neg_row, 1)
            pool.memset(pad, 0.0).then_inc(pad_zero, 1)
            pool.wait_ge(params_in, 16 * PARAMS)
            pool.wait_ge(pad_zero, 1)
            pool.affine_select(out=sgu_wm, in_=sgu_w, compare_op=ALU.is_ge, fill=0.0, base=0,
                               pattern=[[0, SGU_HEADS], [1, P]], channel_multiplier=-1).then_inc(masked, 1)
            pool.wait_ge(line_sb, 1)
            pool.dma_start(scratch_ap, bias_line[0:HEADS, 0, :]).then_inc(line_out, 16)
            pool.wait_ge(line_out, 16)
            for layer in range(2):
                pool.wait_ge(h_ready[2 + 3 * layer], KD)
                pool.dma_start(subk, a["subkeys"][layer]).then_inc(subk_in, 16)
                if layer == 0:
                    pool.wait_ge(y_added, 2)
                    pool.dma_start(hankel, bass.AP(scratch, 0, [[1, P], [REL_SPAN, HEADS], [1, 384]])).then_inc(hankel_in, 16)
                    pool.wait_ge(v1T_ready, 4)

                    def stage(k):
                        for s in range(2):
                            m = 2 * k + s
                            at_least(pool, heads_out, 2 * (m - 2) + 2)
                            pool.tensor_copy(q_st[:, s, :], z1[:, m, :]).then_inc(staged, 1)
                            pool.tensor_copy(k_st[:, s, :], z1[:, 8 + m, :]).then_inc(staged, 1)
                            pool.tensor_copy(v_st[:, s], v1T[:, :, m * P:(m + 1) * P] if isinstance(m, int)
                                             else v1T[:, :, bass.ds(m * P, P)]).then_inc(staged, 1)

                    sweep(pool, HEADS // 4, stage, first=1)

        @block.scalar
        def _(act):
            def round_half(name, k, j, b):
                u = 2 * (TILE0[name] + 4 * k + j) + b
                act.wait_ge(loaded[j % RAW], loaded_count(name, k, j))
                at_least(act, half_used, u - SPLIT + 1)
                s = (2 * j + b) % SPLIT
                act.activation(w_hi[:, s, :], raw[:, j % RAW, b * HALF:(b + 1) * HALF], ACT.Copy).then_inc(hi_ready, 1)

            def ahead(name, k, j):
                if isinstance(k, int) and TILE0[name] + 4 * k + j + 2 >= TILES:
                    return
                for b in range(2):
                    round_half(name, k, j + 2, b)

            def taking(name, take, turns, k0=0, last=0):
                def body(k):
                    for j in range(4):
                        act.wait_ge(half_used, 2 * (TILE0[name] + 4 * (k + k0) + j) + 2)
                        take(k + k0, j)
                        ahead(name, k + k0, j)
                sweep(act, turns, body, last=last)

            def only_ahead(name, turns):
                def body(k):
                    for j in range(4):
                        ahead(name, k, j)
                sweep(act, turns, body)

            def root(r):
                act.wait_ge(rstd_step[r], 2)
                act.activation(rstd[:], ms[:, 1, :], ACT.Sqrt).then_inc(rstd_ready[r], 1)

            def split_operand(s, all_at_once=False):
                for q in range(4):
                    act.wait_ge(h_ready[s], KD if all_at_once else 2 * q + 2)
                    act.activation(x_hi[:, 2 * q:2 * q + 2, :], hT[:, 2 * q:2 * q + 2, :], ACT.Copy).then_inc(x_hi_ready[s], 1)

            for j in range(2):
                for b in range(2):
                    round_half("w_in", 0, j, b)
            act.wait_ge(line_ps, 1)
            act.activation(bias_line[0:HEADS, 0, :], psum[0:HEADS, 0, :], ACT.Copy).then_inc(line_sb, 1)
            root(0)
            split_operand(0)
            taking("w_in", lambda k, j: act.activation(z0[:, j, k, :], proj_ps[j % 2], ACT.Copy).then_inc(proj_taken, 1), 4)
            act.wait_ge(proj_taken, PROJ0["w_out"])
            act.activation(sig, z0[:, 1], ACT.Sigmoid).then_inc(gated, 1)
            for i in (1, 0):
                act.activation(guv[:, i], z0[:, 2 + i], ACT.Gelu_apprx_tanh).then_inc(gated, 1)
            act.wait_ge(ln_step[1], 5)
            act.activation(lnstat[:, 1, 3, :], lnstat[:, 1, 2, :], ACT.Sqrt).then_inc(ln_root[1], 1)
            act.wait_ge(ln_step[1], 9)
            for c in range(KC):
                act.activation(vn[:, c, :], centred[:, 1, c, :], ACT.Identity, scale=small[:, 3, c:c + 1],
                               bias=small[:, 4, c:c + 1]).then_inc(vn_ready, 1)
            for g in range(2):
                act.wait_ge(vT_ps, g + 1)
                act.activation(vT[:, g, :], psum[:, 2 + g, :], ACT.Copy).then_inc(vT_ready, 1)
            act.wait_ge(ln_step[0], 5)
            act.activation(lnstat[:, 0, 3, :], lnstat[:, 0, 2, :], ACT.Sqrt).then_inc(ln_root[0], 1)
            act.wait_ge(ln_step[0], 9)
            for c in range(KC):
                act.activation(hT[:, c, :], centred[:, 0, c, :], ACT.Silu, scale=small[:, 1, c:c + 1],
                               bias=small[:, 2, c:c + 1]).then_inc(h_ready[1], 1)
            split_operand(1, True)
            only_ahead("w_out", 2)

            def experts(l):
                act_q, act_u, act_v = f"q{l}", f"u{l}", f"v{l}"
                root(1 + 2 * l)
                split_operand(2 + 3 * l)

                def take_query(k, j):
                    at_least(act, keys_scored, 16 * l + 4 * k + j - 1)
                    act.activation(qs[:, j % 2, :], proj_ps[j % 2], ACT.Copy).then_inc(proj_taken, 1)

                def take_act(k, j):
                    i = 4 * k + j
                    act.activation(big[:, bass.ds(i * T, T)], proj_ps[j % 2], ACT.Gelu_apprx_tanh).then_inc(proj_taken, 1)

                taking(act_q, take_query, 4) if l else taking_first(act_q, take_query)
                taking(act_u, take_act, PICK_TURNS)
                act.wait_ge(soft_in, l + 1)
                act.activation(tv, ids_f_tmp, ACT.Exp).then_inc(soft_exp, 1)
                taking(act_u, take_act, NKEYS // 4 - PICK_TURNS, k0=PICK_TURNS)

                def round_ag(k, j):
                    i = 4 * k + j + 2
                    if isinstance(i, int) and i >= NKEYS:
                        return
                    act.activation(ag_hi[:, j % 2, :], big[:, bass.ds(i * T, T)], ACT.Copy).then_inc(ag_hi_ready, 1)

                act.wait_ge(act_gated, 64 * (l + 1))
                for j in range(2):
                    act.activation(ag_hi[:, j, :], big[:, j * T:(j + 1) * T], ACT.Copy).then_inc(ag_hi_ready, 1)

                def body(k):
                    for j in range(4):
                        act.wait_ge(half_used, 2 * (TILE0[act_v] + 4 * k + j) + 2)
                        round_ag(k, j)
                        ahead(act_v, k, j)
                sweep(act, NKEYS // 4, body, last=1)

            def taking_first(name, take):
                def body(k):
                    for j in range(4):
                        act.wait_ge(half_used, 2 * (TILE0[name] + 4 * k + j) + 2)
                        take(k, j)
                        ahead(name, k, j)
                sweep(act, 4, body, first=1)

            ids_f_tmp = room(top - 2 * KD * T, UNITS, TOPK)[0]
            experts(0)
            root(2)
            split_operand(3)
            taking("qkv", lambda k, j: act.activation(z1[:, bass.ds(4 * k + j, 1), :].rearrange("p a t -> p (a t)"), proj_ps[j % 2],
                                                      ACT.Copy, scale=HD ** -0.5).then_inc(proj_taken, 1), 2)
            taking("qkv", lambda k, j: act.activation(z1[:, bass.ds(4 * k + j, 1), :].rearrange("p a t -> p (a t)"), proj_ps[j % 2],
                                                      ACT.Copy).then_inc(proj_taken, 1), 4, k0=2)
            for g in range(4):
                act.wait_ge(v1T_ps, g + 1)
                act.activation(v1T[:, g // 2, 512 * (g % 2):512 * (g % 2) + 512], psum[:, g, :], ACT.Copy).then_inc(v1T_ready, 1)

            def softmax(k):
                for s in range(2):
                    for e in range(2):
                        h = 4 * k + 2 * s + e
                        act.wait_ge(soft_step, 4 * h + 2)
                        for t in range(TT):
                            act.activation(expd[:, e, t, :], psum[:, e, t * T:(t + 1) * T], ACT.Exp, bias=soft[:, e, 1, t:t + 1],
                                           accum_out=soft[:, e, 2, t:t + 1]).then_inc(exp_ready, 1)
                        act.wait_ge(probT_ps, h + 1)
                        act.activation(probT[:, e].rearrange("p a b -> p (a b)"), psum[:, 2 + e, 0:3 * P], ACT.Copy).then_inc(probT_ready, 1)
            sweep(act, HEADS // 4, softmax)
            split_operand(4)
            only_ahead("w_o", 2)
            experts(1)
            root(4)

        @block.vector
        def _(dve):
            def lower_half(name, k, j, b):
                u = 2 * (TILE0[name] + 4 * k + j) + b
                dve.wait_ge(hi_ready, u + 1)
                s = (2 * j + b) % SPLIT
                dve.tensor_tensor(w_lo[:, s, :], raw[:, j % RAW, b * HALF:(b + 1) * HALF], w_hi[:, s, :].bitcast(F32),
                                  ALU.subtract).then_inc(split_ready, 1)

            def ahead(name, k, j, last_wait=None):
                if isinstance(k, int) and TILE0[name] + 4 * k + j + 2 >= TILES:
                    return
                for b in range(2):
                    if b and last_wait:
                        dve.wait_ge(*last_wait)
                    lower_half(name, k, j + 2, b)

            def norm(r, gain, s):
                for q in range(4):
                    dve.tensor_tensor(sq[:, 2 * q:2 * q + 2, :], xT[:, 2 * q:2 * q + 2, :], xT[:, 2 * q:2 * q + 2, :],
                                      ALU.mult).then_inc(sq_ready[r], 1)
                dve.wait_ge(ss_ready[r], 1)
                dve.tensor_scalar(ms[:, 0, :], misc_ps[0][:, 0:T], 1.0 / D, EPS, ALU.mult, ALU.add).then_inc(rstd_step[r], 1)
                dve.wait_ge(rstd_step[r], 1)
                dve.reciprocal(ms[:, 1, :], ms[:, 0, :]).then_inc(rstd_step[r], 1)
                dve.wait_ge(rstd_ready[r], 1)
                for m in range(KD):
                    dve.scalar_tensor_tensor(out=hT[:, m, :], in0=xT[:, m, :], scalar=gains[:, gain, m:m + 1], in1=rstd[:],
                                             op0=ALU.mult, op1=ALU.mult).then_inc(h_ready[s], 1)
                if s < 6:
                    split_operand(s)

            def split_operand(s):
                for q in range(4):
                    dve.wait_ge(x_hi_ready[s], q + 1)
                    dve.tensor_tensor(x_lo[:, 2 * q:2 * q + 2, :], hT[:, 2 * q:2 * q + 2, :],
                                      x_hi[:, 2 * q:2 * q + 2, :].bitcast(F32), ALU.subtract).then_inc(operand_ready[s], 1)

            def layer_norm(i, src):
                step, st = ln_step[i], lnstat[:, i]
                dve.wait_ge(ln_sum[i], 1)
                dve.tensor_scalar(st[:, 0, :], misc_ps[i][:, 0:T], 1.0 / CH, None, ALU.mult).then_inc(step, 1)
                dve.wait_ge(step, 1)
                dve.tensor_tensor(centred[:, i], src, st[:, 0:1, :].to_broadcast([P, KC, T]), ALU.subtract).then_inc(step, 1)
                dve.wait_ge(step, 2)
                dve.tensor_tensor(lnsq[:, i], centred[:, i], centred[:, i], ALU.mult).then_inc(step, 1)
                dve.wait_ge(ln_sum[i], 2)
                dve.tensor_scalar(st[:, 1, :], misc_ps[i][:, 0:T], 1.0 / CH, EPS, ALU.mult, ALU.add).then_inc(step, 1)
                dve.wait_ge(step, 4)
                dve.reciprocal(st[:, 2, :], st[:, 1, :]).then_inc(step, 1)
                dve.wait_ge(ln_root[i], 1)
                for c in range(KC):
                    dve.tensor_tensor(centred[:, i, c, :], centred[:, i, c, :], st[:, 3, :], ALU.mult).then_inc(step, 1)

            for j in range(2):
                for b in range(2):
                    lower_half("w_in", 0, j, b)
            dve.wait_ge(params_in, 16 * PARAMS)
            dve.wait_ge(x_in, 16)
            norm(0, 0, 0)
            sweep(dve, 4, lambda k: [ahead("w_in", k, j) for j in range(4)])
            dve.wait_ge(gated, 1)
            dve.wait_ge(pad_zero, 1)
            dve.tensor_tensor(pad[:, :, CONV - 1:CONV - 1 + T], z0[:, 0], sig, ALU.mult).then_inc(pad_ready, 1)
            layer_norm(1, guv[:, 1])
            dve.wait_ge(pad_ready, 1)
            for c in range(KC):
                dve.tensor_scalar(conv[:, c, :], pad[:, c, 0:T], conv_w[:, c, 0:1], small[:, 0, c:c + 1],
                                  ALU.mult, ALU.add).then_inc(conv_step, 1)
            with dve.Fori(1, CONV) as tap:
                for c in range(KC):
                    dve.wait_ge(conv_step, KC * tap + c - KC + 1)
                    dve.scalar_tensor_tensor(out=conv[:, c, :], in0=pad[:, c, bass.ds(tap, T)], scalar=conv_w[:, c, bass.ds(tap, 1)],
                                             in1=conv[:, c, :], op0=ALU.mult, op1=ALU.add).then_inc(conv_step, 1)
            dve.wait_ge(conv_step, KC * CONV)
            layer_norm(0, conv)
            for c in range(KC):
                dve.wait_ge(mixed, c + 1)
                dve.tensor_tensor(hT[:, KC + c, :], guv[:, 0, c, :], psum[:, c // 2, (c % 2) * T:(c % 2 + 1) * T],
                                  ALU.mult).then_inc(h_ready[1], 1)
            split_operand(1)

            def add_residual(name):
                def body(k):
                    for j in range(4):
                        dve.wait_ge(half_used, 2 * (TILE0[name] + 4 * k + j) + 2)
                        x_m = xT[:, bass.ds(4 * k + j, 1), :].rearrange("p a t -> p (a t)")
                        dve.tensor_tensor(x_m, x_m, proj_ps[j % 2], ALU.add).then_inc(proj_taken, 1)
                        ahead(name, k, j)
                sweep(dve, 2, body)

            def rank_keys(l, r, slot, between):
                s0 = 13 * (16 * l + r)
                sti = st_i.bitcast(U32)
                results = []
                for src, dst in ((st_v, topv), (sti, topi)):
                    dst = dst.rearrange("p (t h) a r -> p t (h a) r", t=TT)
                    for o in (0, 8):
                        results.append((dst[:, :, bass.ds(r, 1), o:o + 8], src[:, :, o:o + 8].rearrange("p t (a r) -> p t a r", a=1)))
                dve.wait_ge(keys_scored, 16 * l + r + 1)
                dve.tensor_copy(st_s.rearrange("p t s -> p (t s)"), misc_ps[slot][:, 0:T]).then_inc(scores_copied, 1)
                between(16 * l + r + 1)
                for t in range(TT):
                    dve.max(st_v[:, t, 0:8], st_s[:, t, :]).then_inc(rank_step, 1)
                dve.wait_ge(rank_step, s0 + 2)
                dve.tensor_copy(*results[0]).then_inc(rank_step, 1)
                for t in range(TT):
                    dve.max_index(sti[:, t, 0:8], st_v[:, t, 0:8], st_s[:, t, :]).then_inc(rank_step, 1)
                for t in range(TT):
                    dve.match_replace(st_w[:, t, :], st_v[:, t, 0:8], st_s[:, t, :], LOWEST).then_inc(rank_step, 1)
                dve.wait_ge(rank_step, s0 + 7)
                dve.tensor_copy(*results[2]).then_inc(rank_step, 1)
                for t in range(TT):
                    dve.max(st_v[:, t, 8:16], st_w[:, t, :]).then_inc(rank_step, 1)
                dve.wait_ge(rank_step, s0 + 10)
                dve.tensor_copy(*results[1]).then_inc(rank_step, 1)
                for t in range(TT):
                    dve.max_index(sti[:, t, 8:16], st_v[:, t, 8:16], st_w[:, t, :]).then_inc(rank_step, 1)
                dve.wait_ge(rank_step, s0 + 13)
                dve.tensor_copy(*results[3]).then_inc(ranked, 1)

            def build_candidates(l):
                b0 = 23 * l
                dve.wait_ge(ranked, 16 * (l + 1))
                dve.wait_ge(rank_step, 13 * 16 * (l + 1))
                dve.tensor_scalar(topi[:, :, 0, :], topi[:, :, 0, :], float(NKEYS), None, ALU.mult).then_inc(build_step, 1)
                dve.wait_ge(build_step, b0 + 1)
                for src, dst in ((topv, cand), (topi, cid)):
                    for i0, rows, n in ROW_GROUPS:
                        o = dst[:, :, ROW_AT[i0]:ROW_AT[i0] + rows * n]
                        first, second = src[:, :, 0, i0:i0 + rows], src[:, :, 1, 0:n]
                        if rows == 1:
                            first = first.to_broadcast([P, UNITS, n])
                        elif n == 1:
                            second = second.to_broadcast([P, UNITS, rows])
                        else:
                            o = o.rearrange("p u (r n) -> p u r n", n=n)
                            first = first.rearrange("p u (r n) -> p u r n", n=1).to_broadcast([P, UNITS, rows, n])
                            second = second.rearrange("p u (r n) -> p u r n", r=1).to_broadcast([P, UNITS, rows, n])
                        dve.tensor_tensor(o, first, second, ALU.add).then_inc(build_step, 1)

            def stage_pair(k):
                dve.tensor_copy(cst, cand[:, bass.ds(2 * k, 2), :]).then_inc(pick_step, 1)

            def pick(l, k):
                s0 = 21 * (8 * l + k) + l + 1
                pos = pi.bitcast(U32)
                for e in range(2):
                    dve.max(pv[:, e, 0:8], cst[:, e, :]).then_inc(pick_step, 1)
                dve.wait_ge(pick_step, s0 + 2)
                dve.tensor_copy(tv[:, bass.ds(2 * k, 2), 0:8], pv[:, :, 0:8]).then_inc(pick_step, 1)
                for e in range(2):
                    dve.max_index(pos[:, e, 0:8], pv[:, e, 0:8], cst[:, e, :]).then_inc(pick_step, 1)
                for e in range(2):
                    dve.match_replace(cwk[:, e, :], pv[:, e, 0:8], cst[:, e, :], LOWEST).then_inc(pick_step, 1)
                dve.wait_ge(pick_step, s0 + 7)
                dve.tensor_copy(pf[:, :, 0:8], pos[:, :, 0:8]).then_inc(pick_step, 1)
                for e in range(2):
                    dve.max(pv[:, e, 8:16], cwk[:, e, :]).then_inc(pick_step, 1)
                dve.wait_ge(pick_step, s0 + 10)
                dve.tensor_copy(tv[:, bass.ds(2 * k, 2), 8:16], pv[:, :, 8:16]).then_inc(pick_step, 1)
                for e in range(2):
                    dve.max_index(pos[:, e, 8:16], pv[:, e, 8:16], cwk[:, e, :]).then_inc(pick_step, 1)
                if not (isinstance(k, int) and k == UNITS // 2 - 1):
                    stage_pair(k + 1)
                else:
                    dve.tensor_copy(cst, cst).then_inc(pick_step, 1)
                dve.wait_ge(pick_step, s0 + 13)
                dve.tensor_copy(pf[:, :, 8:16], pos[:, :, 8:16]).then_inc(pick_step, 1)
                dve.wait_ge(pick_step, s0 + 15)
                places = iota[:, 0:CANDS].rearrange("p (r c) -> p r c", r=1).to_broadcast([P, TOPK, CANDS])
                for e in range(2):
                    dve.tensor_tensor(eq[:, e], pf[:, e, :].rearrange("p (r c) -> p r c", c=1).to_broadcast([P, TOPK, CANDS]),
                                      places, ALU.is_equal).then_inc(pick_step, 1)
                for e in range(2):
                    dve.wait_ge(pick_step, s0 + 16 + e)
                    number = cid[:, bass.ds(2 * k + e, 1), :].to_broadcast([P, TOPK, CANDS])
                    dve.tensor_tensor(eq[:, e], eq[:, e], number, ALU.mult).then_inc(pick_step, 1)
                for e in range(2):
                    dve.wait_ge(pick_step, s0 + 18 + e)
                    dve.tensor_reduce(ids[:, bass.ds(2 * k + e, 1), :].rearrange("p a r -> p (a r)"), eq[:, e], AX, ALU.add)\
                       .then_inc(pick_step, 1)

            def finish_picks(l):
                b0 = 23 * l + 15
                diff = room(top - 2 * KD * T, UNITS, TOPK)[0]
                dve.wait_ge(pick_step, (21 * 8 + 1) * (l + 1))
                dve.tensor_tensor(diff, tv, tv[:, :, 0:1].to_broadcast([P, UNITS, TOPK]), ALU.subtract).then_inc(soft_in, 1)
                ii = id_i.bitcast(I32)
                dve.tensor_copy(ii[:, 0, :], ids.rearrange("p u r -> p (u r)")).then_inc(build_step, 1)
                dve.wait_ge(build_step, b0 + 1)
                dve.tensor_scalar(ii[:, 1, :], ii[:, 0, :], 7, None, ALU.logical_shift_right).then_inc(build_step, 1)
                dve.tensor_scalar(ii[:, 2, :], ii[:, 0, :], NKEYS - 1, None, ALU.bitwise_and).then_inc(build_step, 1)
                dve.wait_ge(build_step, b0 + 3)
                dve.tensor_copy(id_f.rearrange("p a u r -> p a (u r)"), ii[:, 1:3, :]).then_inc(build_step, 1)
                dve.wait_ge(soft_exp, l + 1)
                dve.tensor_reduce(gsum[:, 0, :], tv, AX, ALU.add).then_inc(build_step, 1)
                dve.wait_ge(build_step, b0 + 5)
                dve.reciprocal(gsum[:, 1, :], gsum[:, 0, :]).then_inc(build_step, 1)
                dve.wait_ge(build_step, b0 + 6)
                dve.tensor_tensor(tv, tv, gsum[:, 1, :].rearrange("p (u r) -> p u r", r=1).to_broadcast([P, UNITS, TOPK]),
                                  ALU.mult).then_inc(build_step, 1)
                dve.wait_ge(picks_ps, l + 1)
                dve.tensor_copy(picks[:, 0:2, :].rearrange("p a t -> p (a t)"), psum[:, 0, :]).then_inc(picks_ready, 1)
                dve.tensor_copy(picks[:, 2, :], psum[:, 1, 0:T]).then_inc(build_step, 1)
                dve.wait_ge(picks_ready, l + 1)
                dve.wait_ge(build_step, b0 + 8)

            def one_hots(l, g, half):
                for i in range(4):
                    s = 4 * half + i
                    at_least(dve, scattered, T * l + 4 * g + i - 7)
                    dve.tensor_scalar(hot_j[:, s, :], iota, picks[:, 1, bass.ds(4 * g + i, 1)], None, ALU.is_equal).then_inc(hot_ready, 1)
                    dve.tensor_scalar(hot_i[:, s, :], iota, picks[:, 0, bass.ds(4 * g + i, 1)], picks[:, 2, bass.ds(4 * g + i, 1)],
                                      ALU.is_equal, ALU.mult).then_inc(hot_ready, 1)

            table = big[:].rearrange("p (i t) -> p i t", t=T)

            def apply_gates(l, g, half):
                dve.wait_ge(scattered, T * l + 4 * g + 4)
                block_ = table[:, :, bass.ds(4 * g, 4)]
                dve.tensor_tensor(block_, block_, misc_ps[half].rearrange("p (t i) -> p i t", t=4), ALU.mult).then_inc(act_gated, 1)

            def experts(l):
                q, u, v = f"q{l}", f"u{l}", f"v{l}"
                norm(1 + 2 * l, 2 * l + 1, 2 + 3 * l)

                def q_body(k):
                    for j in range(4):
                        if isinstance(k, int) and 4 * k + j == 0:
                            ahead(q, k, j)
                        else:
                            rank_keys(l, 4 * k + j - 1, (j - 1) % 2, lambda copied: ahead(q, k, j, last_wait=(scores_copied, copied)))

                sweep(dve, 4, q_body, first=1)
                rank_keys(l, 15, 1, lambda copied: dve.wait_ge(scores_copied, copied))
                build_candidates(l)
                dve.wait_ge(build_step, 23 * l + 15)
                stage_pair(0)

                def u_body(k):
                    for j in range(4):
                        ahead(u, k, j, last_wait=(pick_step, (21 * 8 + 1) * l + 21 * k + 1) if j == 3 else None)
                    pick(l, k)

                sweep(dve, PICK_TURNS - 1, u_body, first=0 if l else 1, last=1)
                for j in range(4):
                    ahead(u, PICK_TURNS - 1, j)
                finish_picks(l)
                with dve.Fori(PICK_TURNS, NKEYS // 4) as k:
                    for j in range(4):
                        ahead(u, k, j)
                dve.wait_ge(proj_taken, PROJ0[u] + NKEYS)
                one_hots(l, 0, 0)

                def g_body(k):
                    one_hots(l, 2 * k + 1, 1)
                    apply_gates(l, 2 * k, 0)
                    if not (isinstance(k, int) and k == 31):
                        one_hots(l, 2 * k + 2, 0)
                    apply_gates(l, 2 * k + 1, 1)
                sweep(dve, 32, g_body, first=0 if l else 1, last=1)

                def lower_ag(k, j):
                    i = 4 * k + j + 2
                    if isinstance(i, int) and i >= NKEYS:
                        return
                    dve.wait_ge(ag_hi_ready, NKEYS * l + i + 1)
                    dve.tensor_tensor(ag_lo[:, j % 2, :], big[:, bass.ds(i * T, T)], ag_hi[:, j % 2, :].bitcast(F32),
                                      ALU.subtract).then_inc(ag_ready, 1)

                for j in range(2):
                    lower_ag(0, j - 2)

                def v_body(k):
                    for j in range(4):
                        lower_ag(k, j)
                        ahead(v, k, j)
                sweep(dve, NKEYS // 4, v_body, last=1)
                dve.wait_ge(half_used, 2 * (TILE0[v] + NKEYS))
                for b in range(2):
                    dve.tensor_tensor(xT[:, 4 * b:4 * b + 4, :], xT[:, 4 * b:4 * b + 4, :], y_ps[:, 4 * b:4 * b + 4, :],
                                      ALU.add).then_inc(y_added, 1)
                dve.wait_ge(y_added, 2 * (l + 1))

            add_residual("w_out")
            dve.wait_ge(proj_taken, PROJ0["q0"])
            experts(0)
            norm(2, 2, 3)
            sweep(dve, 6, lambda k: [ahead("qkv", k, j) for j in range(4)])

            def softmax(k):
                for s in range(2):
                    m = 2 * k + s
                    for e in range(2):
                        h = 2 * m + e
                        dve.wait_ge(scores_ready, h + 1)
                        at_least(dve, soft_step, 4 * h)
                        dve.tensor_reduce(soft[:, e, 0, :], psum[:, e, :].rearrange("p (t s) -> p t s", t=TT), AX, ALU.max).then_inc(soft_step, 1)
                        dve.wait_ge(soft_step, 4 * h + 1)
                        dve.tensor_scalar(soft[:, e, 1, :], soft[:, e, 0, :], -1.0, None, ALU.mult).then_inc(soft_step, 1)
                        dve.wait_ge(exp_ready, 2 * h + 2)
                        dve.reciprocal(soft[:, e, 3, :], soft[:, e, 2, :]).then_inc(soft_step, 1)
                        dve.wait_ge(soft_step, 4 * h + 3)
                        dve.tensor_tensor(prob[:, e], expd[:, e],
                                          soft[:, e, 3, :].rearrange("p (t s) -> p t s", s=1).to_broadcast([P, TT, T]),
                                          ALU.mult).then_inc(soft_step, 1)
                    dve.wait_ge(heads_out, 2 * m + 2)
                    dve.tensor_copy(hT[:, bass.ds(m, 1), :].rearrange("p a t -> p (a t)"), misc_ps[s][:, 0:T]).then_inc(h_ready[4], 1)
            sweep(dve, HEADS // 4, softmax, first=1)
            split_operand(4)
            add_residual("w_o")
            dve.wait_ge(proj_taken, PROJ0["q1"])
            experts(1)
            norm(4, 4, 6)

        @block.tensor
        def _(pe):
            def project(name, k, j):
                n, p = TILE0[name] + 4 * k + j, PROJ0[name] + 4 * k + j
                at_least(pe, proj_taken, p - 1)
                for b in range(2):
                    pe.wait_ge(split_ready, 2 * n + b + 1)
                    s = (2 * j + b) % SPLIT
                    for i in range(4):
                        m = 4 * b + i
                        hi, lo = (w[:, s, i * P:(i + 1) * P] for w in (w_hi, w_lo))
                        pe.matmul(proj_ps[j % 2], hi, x_hi[:, m, :], start=(m == 0), stop=False)
                        pe.matmul(proj_ps[j % 2], hi, x_lo[:, m, :], start=False, stop=False)
                        mm = pe.matmul(proj_ps[j % 2], lo, x_hi[:, m, :], start=False, stop=(m == KD - 1))
                    mm.then_inc(half_used, 1)

            def projections(name, tiles, first=0):
                sweep(pe, tiles // 4, lambda k: [project(name, k, j) for j in range(4)], first=first)

            def sum_squares(r):
                for m in range(KD):
                    pe.wait_ge(sq_ready[r], m // 2 + 1)
                    mm = pe.matmul(misc_ps[0][:, 0:T], ones, sq[:, m, :], start=(m == 0), stop=(m == KD - 1))
                mm.then_inc(ss_ready[r], 1)

            pe.wait_ge(params_in, 16 * PARAMS)
            pe.wait_ge(neg_row, 1)
            pe.matmul(psum[0:HEADS, 0, :], rel[0:REL_BUCKETS + 1, 0, :], line[0:REL_BUCKETS + 1, 0, :],
                      start=True, stop=True).then_inc(line_ps, 1)
            sum_squares(0)
            pe.wait_ge(operand_ready[0], 4)
            projections("w_in", 16, first=1)

            def channel_sum(i, src):
                for c in range(KC):
                    mm = pe.matmul(misc_ps[i][:, 0:T], ones, src[:, c, :], start=(c == 0), stop=(c == KC - 1))
                mm.then_inc(ln_sum[i], 1)

            pe.wait_ge(gated, 2)
            channel_sum(1, guv[:, 1])
            pe.wait_ge(ln_step[1], 3)
            channel_sum(1, lnsq[:, 1])
            pe.wait_ge(vn_ready, KC)
            for t in range(TT):
                for c in range(KC):
                    mm = pe.transpose(psum[:, 2 + t, c * P:(c + 1) * P], vn[:, c, t * P:(t + 1) * P], ident)
                mm.then_inc(vT_ps, 1)
            pe.wait_ge(vT_ready, TT)
            pe.wait_ge(masked, 1)
            pe.wait_ge(line_sb, 1)
            for c in range(KC):
                for t in range(TT):
                    for e in range(2):
                        h = 2 * c + e
                        o = psum[HD * e:HD * (e + 1), c // 2, (c % 2) * T + t * P:(c % 2) * T + (t + 1) * P]
                        pe.matmul(o, vT[:, t, h * HD:(h + 1) * HD], sgu_wm[:, h, :], start=True, stop=False)
                        mm = pe.matmul(o, ones[0:1, 0:HD], sgu_b[0:1, h, :], start=False, stop=True)
                mm.then_inc(mixed, 1)
            pe.wait_ge(conv_step, KC * CONV)
            channel_sum(0, conv)
            pe.wait_ge(ln_step[0], 3)
            channel_sum(0, lnsq[:, 0])
            pe.wait_ge(operand_ready[1], 4)
            projections("w_out", 8)

            def score_keys(l, k, j):
                r = 16 * l + 4 * k + j
                pe.wait_ge(proj_taken, PROJ0[f"q{l}"] + 4 * k + j + 1)
                at_least(pe, ranked, r - 1)
                s = j % 2
                for t in range(TT):
                    mm = pe.matmul(misc_ps[s][:, t * P:(t + 1) * P], qs[:, s, t * P:(t + 1) * P],
                                   subk[:, bass.ds(4 * k + j, 1), :].rearrange("p a b -> p (a b)"), start=True, stop=True)
                mm.then_inc(keys_scored, 1)

            def experts(l):
                q, u, v = f"q{l}", f"u{l}", f"v{l}"
                sum_squares(1 + 2 * l)
                pe.wait_ge(operand_ready[2 + 3 * l], 4)
                pe.wait_ge(subk_in, 16 * (l + 1))

                def q_body(k):
                    for j in range(4):
                        project(q, k, j)
                        if not (isinstance(k, int) and 4 * k + j == 0):
                            score_keys(l, k, j - 1) if j else score_keys(l, k - 1, 3)
                sweep(pe, 4, q_body, first=1)
                score_keys(l, 3, 3)
                projections(u, 4 * PICK_TURNS)
                pe.wait_ge(build_step, 23 * l + 15 + 7)
                for a_, src in enumerate((id_f[:, 0], id_f[:, 1], tv)):
                    for t in range(TT):
                        at = (a_ * TT + t) * P
                        mm = pe.transpose(psum[:, at // 512, at % 512:at % 512 + P],
                                          src.rearrange("p (t u) r -> p t (u r)", t=TT)[:, t, :], ident)
                mm.then_inc(picks_ps, 1)
                with pe.Fori(PICK_TURNS, NKEYS // 4) as k:
                    for j in range(4):
                        project(u, k, j)

                def scatter(k):
                    for half in range(2):
                        g = 2 * k + half
                        at_least(pe, act_gated, 64 * l + g - 1)
                        for i in range(4):
                            pe.wait_ge(hot_ready, 2 * (T * l + 4 * g + i) + 2)
                            s = 4 * half + i
                            pe.matmul(misc_ps[half][:, i * P:(i + 1) * P], hot_j[:, s, :], hot_i[:, s, :],
                                      start=True, stop=True).then_inc(scattered, 1)
                sweep(pe, 32, scatter, first=0 if l else 1)

                def combine(k):
                    for j in range(4):
                        n, i = TILE0[v] + 4 * k + j, 4 * k + j
                        pe.wait_ge(ag_ready, NKEYS * l + i + 1)
                        begin, end = isinstance(i, int) and i == 0, isinstance(i, int) and i == NKEYS - 1
                        for b in range(2):
                            pe.wait_ge(split_ready, 2 * n + b + 1)
                            s = (2 * j + b) % SPLIT
                            for c in range(4):
                                m = 4 * b + c
                                hi, lo = (w[:, s, c * P:(c + 1) * P] for w in (w_hi, w_lo))
                                pe.matmul(y_ps[:, m, :], hi, ag_hi[:, j % 2, :], start=begin and m % 2 == 0, stop=False, skip_group_check=True)
                                pe.matmul(y_ps[:, m, :], hi, ag_lo[:, j % 2, :], start=False, stop=False, skip_group_check=True)
                                mm = pe.matmul(y_ps[:, m, :], lo, ag_hi[:, j % 2, :], start=False, stop=end, skip_group_check=True)
                            mm.then_inc(half_used, 1)
                sweep(pe, NKEYS // 4, combine, first=1, last=1)

            experts(0)
            sum_squares(2)
            pe.wait_ge(operand_ready[3], 4)
            projections("qkv", 24)
            pe.wait_ge(proj_taken, PROJ0["w_o"])
            for t in range(TT):
                for g in range(2):
                    for i in range(4):
                        mm = pe.transpose(psum[:, 2 * t + g, i * P:(i + 1) * P], z1[:, 16 + 4 * g + i, t * P:(t + 1) * P], ident)
                    mm.then_inc(v1T_ps, 1)
            pe.wait_ge(v1T_ready, 4)
            pe.wait_ge(hankel_in, 16)

            def attend(k):
                for s in range(2):
                    m = 2 * k + s
                    pe.wait_ge(staged, 3 * m + 3)
                    for e in range(2):
                        h = 2 * m + e
                        at_least(pe, exp_ready, 2 * (h - 2) + 2)
                        for t in range(TT):
                            o = psum[:, e, t * T:(t + 1) * T]
                            pe.matmul(o, q_st[HD * e:HD * (e + 1), s, t * P:(t + 1) * P],
                                      k_st[HD * e:HD * (e + 1), s, :], start=True, stop=False)
                            mm = pe.matmul(o, anti, hankel[:, bass.ds(h, 1), (TT - 1 - t) * P:(TT - 1 - t) * P + T].rearrange("p a t -> p (a t)"),
                                           start=False, stop=True)
                        mm.then_inc(scores_ready, 1)
                    for e in range(2):
                        h = 2 * m + e
                        pe.wait_ge(soft_step, 4 * h + 4)
                        at_least(pe, probT_ready, h - 1)
                        for i, (t, c) in enumerate(((0, 0), (1, 0), (1, 1))):
                            mm = pe.transpose(psum[:, 2 + e, i * P:(i + 1) * P], prob[:, e, t, c * P:(c + 1) * P], ident)
                        mm.then_inc(probT_ps, 1)
                    at_least(pe, h_ready[4], m - 1)
                    for e in range(2):
                        h = 2 * m + e
                        pe.wait_ge(probT_ready, h + 1)
                        o = misc_ps[s][HD * e:HD * (e + 1), 0:T]
                        pe.matmul(o, v_st[:, s, 0, HD * e:HD * (e + 1)], probT[:, e, 0:2, :].rearrange("p a b -> p (a b)"),
                                  start=True, stop=False, skip_group_check=True)
                        pe.matmul(o[:, P:T], v_st[:, s, 1, HD * e:HD * (e + 1)], probT[:, e, 2, :],
                                  start=False, stop=True, skip_group_check=True).then_inc(heads_out, 1)
            sweep(pe, HEADS // 4, attend, first=1)
            pe.wait_ge(operand_ready[4], 4)
            projections("w_o", 8)
            experts(1)
            sum_squares(4)


def kernel(x, ev_w_in, ev_conv_w, ev_conv_b, ev_conv_ln_g, ev_conv_ln_b, ev_sgu_ln_g, ev_sgu_ln_b, ev_sgu_w, ev_sgu_b,
           ev_w_out, od_w_qkv, od_w_o, rel_bias, peer_w_q, peer_subkeys, peer_u, peer_v,
           norm_mix_g, norm_ffn_g, norm_final_g):
    import concourse.bacc as bacc
    from concourse.bass_utils import run_bass_kernel_spmd

    f = np.asarray

    def tiles(w):
        return np.ascontiguousarray(f(w).reshape(KD, P, -1, P).transpose(2, 1, 0, 3)).reshape(-1, P, D)

    def columns(v, n):
        return np.ascontiguousarray(f(v).reshape(n, P).T)

    w_in = tiles(ev_w_in[0])
    w_in = np.ascontiguousarray(w_in.reshape(4, KC, P, D).transpose(1, 0, 2, 3)).reshape(-1, P, D)
    const, line = constants()
    gains = np.stack([columns(g, KD) for g in (norm_mix_g[0], norm_ffn_g[0], norm_mix_g[1], norm_ffn_g[1], norm_final_g)], 1)
    small = np.stack([columns(g[0], KC) for g in (ev_conv_b, ev_conv_ln_g, ev_conv_ln_b, ev_sgu_ln_g, ev_sgu_ln_b)], 1)
    arrays = {
        "xT": np.ascontiguousarray(f(x)[0].T),
        "w_in": w_in, "w_out": tiles(ev_w_out[0]), "w_qkv": tiles(od_w_qkv[0]), "w_o": tiles(od_w_o[0]),
        "peer_q0": tiles(peer_w_q[0]), "peer_q1": tiles(peer_w_q[1]),
        "peer_u0": tiles(f(peer_u[0]).T), "peer_u1": tiles(f(peer_u[1]).T),
        "peer_v0": f(peer_v[0]).reshape(NKEYS, P, D), "peer_v1": f(peer_v[1]).reshape(NKEYS, P, D),
        "subkeys": np.ascontiguousarray(f(peer_subkeys).reshape(2, 2 * PEER_HEADS, NKEYS, P).transpose(0, 3, 1, 2)),
        "const": const, "line": line, "gains": gains, "small": small,
        "conv_w": np.ascontiguousarray(f(ev_conv_w[0]).reshape(CONV, KC, P).transpose(2, 1, 0)),
        "rel": f(rel_bias),
        "sgu_w": np.ascontiguousarray(f(ev_sgu_w[0]).transpose(2, 0, 1)),
        "sgu_b": f(ev_sgu_b[0]).reshape(1, SGU_HEADS, P),
    }
    nc = bacc.Bacc("TRN2", target_bir_lowering=False, num_devices=1)
    arrays = {f"in_{n}": v for n, v in arrays.items()}
    given = {n[3:]: nc.dram_tensor(n, v.shape, F32, kind="ExternalInput").ap() for n, v in arrays.items()}
    out = nc.dram_tensor("out", (D, T), F32, kind="ExternalOutput").ap()
    for n in ("peer_q", "peer_u", "peer_v"):
        given[n] = [given[f"{n}{l}"] for l in range(2)]
    build(nc, given, out)
    r = run_bass_kernel_spmd(nc, [arrays], core_ids=[0])
    return np.ascontiguousarray(r.results[0]["out"].T).reshape(1, T, D)
```

```python
import math
from contextlib import ExitStack

import concourse.bass as bass
import numpy as np
from concourse import mybir

F32 = mybir.dt.float32
F32R = mybir.dt.float32r
I32 = mybir.dt.int32
U32 = mybir.dt.uint32
ALU = mybir.AluOpType
ACT = mybir.ActivationFunctionType
AX = mybir.AxisListType.X

P = 128
T = 256
TT = T // P
D = 1024
KD = D // P
HALF = D // 2
CONV = 31
CH = 512
KC = CH // P
SGU_HEADS = 8
HEADS = 16
HD = 64
NKEYS = 128
PEER_HEADS = 8
TOPK = 16
UNITS = TT * PEER_HEADS
EPS = 1e-6
NEG = -1e30
LOWEST = -3.0e38
REL_BUCKETS = 32
REL_SPAN = 512
ROWS = [TOPK // (i + 1) for i in range(TOPK)]
ROW_AT = [sum(ROWS[:i]) for i in range(TOPK)]
CANDS = sum(ROWS)
ROW_GROUPS = [(0, 1, 16), (1, 1, 8), (2, 1, 5), (3, 1, 4), (4, 1, 3), (5, 3, 2), (8, 8, 1)]

STREAM = [("w_in", 16, True), ("w_out", 8, True), ("q0", 16, True), ("u0", NKEYS, True), ("v0", NKEYS, False),
          ("qkv", 24, True), ("w_o", 8, True), ("q1", 16, True), ("u1", NKEYS, True), ("v1", NKEYS, False)]
TILE0, PROJ0 = {}, {}
_n = _p = 0
for _name, _tiles, _proj in STREAM:
    TILE0[_name], PROJ0[_name] = _n, _p
    _n += _tiles
    _p += _tiles if _proj else 0
TILES = _n
PARAMS = 8
RAW = 4
SPLIT = 4

PICK_TURNS = UNITS // 2 + 1
LATE_TURN = PICK_TURNS + 8
LATE = 4 * LATE_TURN
GROUPS = T // 4


def bucket_of_distance():
    exact, span = REL_BUCKETS // 2, 2048
    out = []
    for n in range(T):
        if n < exact:
            out.append(n)
        else:
            f = np.float32(np.log(np.float32(n) / np.float32(exact))) / np.float32(math.log(span / exact))
            out.append(min(exact + int(np.float32(f * np.float32(REL_BUCKETS - exact))), REL_BUCKETS - 1))
    return out


def constants():
    c = np.zeros((P, 4 * P), np.float32)
    c[:, 0:P] = np.eye(P)
    c[:, P:2 * P] = np.eye(P)[::-1]
    c[:, 2 * P:3 * P] = 1.0
    c[:, 3 * P:4 * P] = np.arange(P)
    line = np.zeros((REL_BUCKETS + 1, REL_SPAN), np.float32)
    buckets = bucket_of_distance()
    for x in range(REL_SPAN):
        line[buckets[T - 1 - x] if x < T else REL_BUCKETS, x] = 1.0
    return c, line


def at_least(eng, sem, value):
    if not isinstance(value, int) or value > 0:
        eng.wait_ge(sem, value)


def sweep(eng, turns, body, first=0, last=0):
    for k in range(first):
        body(k)
    if turns - last > first:
        with eng.Fori(first, turns - last) as k:
            body(k)
    for k in range(turns - last, turns):
        body(k)


def sweep_from(eng, start, end, body, first=0):
    for k in range(start, start + first):
        body(k)
    with eng.Fori(start + first, end) as k:
        body(k)


def build(nc, a, out):
    ctx = ExitStack()
    with ctx:
        def sb(name, shape, dt=F32):
            return ctx.enter_context(nc.sbuf_tensor(name, shape, dt))

        def sem(name):
            return ctx.enter_context(nc.semaphore(name))

        big = sb("big", [P, NKEYS * T])
        xT = sb("xT", [P, KD, T])
        x_hi = sb("x_hi", [P, KD, T], F32R)
        x_lo = sb("x_lo", [P, KD, T], F32R)
        raw = sb("raw", [P, RAW, D])
        w_hi = sb("w_hi", [P, SPLIT, HALF], F32R)
        w_lo = sb("w_lo", [P, SPLIT, HALF], F32R)
        picks = sb("picks", [P, 3, T])
        hot_j = sb("hot_j", [P, 8, P])
        hot_i = sb("hot_i", [P, 8, P])
        fresh = sb("fresh", [P, 2, T])
        ag_hi = sb("ag_hi", [P, 2, T], F32R)
        ag_lo = sb("ag_lo", [P, 2, T], F32R)
        const = sb("const", [P, 4 * P])
        gains = sb("gains", [P, 5, KD])
        small = sb("small", [P, 6, KC])
        rstd = sb("rstd", [P, T])
        ident, anti, ones, iota = (const[:, P * i:P * (i + 1)] for i in range(4))

        psum = ctx.enter_context(nc.psum_tensor("psum", [P, 8, 512], F32))
        y_ps = psum[:, 0:4, :].rearrange("p b (m t) -> p (b m) t", t=T)
        proj_ps = [psum[:, 4 + i, 0:T] for i in range(2)]
        misc_ps = [psum[:, 6 + i, :] for i in range(2)]

        def room(at, *shape):
            n = math.prod(shape)
            v = big[:, at:at + n]
            if len(shape) == 2:
                v = v.rearrange("p (a b) -> p a b", b=shape[1])
            if len(shape) == 3:
                v = v.rearrange("p (a b c) -> p a b c", b=shape[1], c=shape[2])
            if len(shape) == 4:
                v = v.rearrange("p (a b c d) -> p a b c d", b=shape[1], c=shape[2], d=shape[3])
            return v, at + n

        top = NKEYS * T
        hT, _ = room(top - KD * T, KD, T)
        sq, _ = room(top - 2 * KD * T, KD, T)
        ms, _ = room(top - 2 * KD * T - 2 * T, 2, T)
        z0, at = room(0, 4, KC, T)
        sig, at = room(at, KC, T)
        guv, at = room(at, 2, KC, T)
        pad, at = room(at, KC, 288)
        conv, at = room(at, KC, T)
        centred, at = room(at, 2, KC, T)
        lnsq, at = room(at, 2, KC, T)
        lnstat, at = room(at, 2, 4, T)
        vn, at = room(at, KC, T)
        vT, at = room(at, TT, CH)
        sgu_w, at = room(at, SGU_HEADS, P)
        sgu_wm, at = room(at, SGU_HEADS, P)
        sgu_b, at = room(at, SGU_HEADS, P)
        conv_w, at = room(at, KC, CONV)
        taps, at = room(at, 2, P)
        rel, at = room(at, 1, HEADS)
        line, at = room(at, 1, REL_SPAN)
        bias_line, at = room(at, 1, REL_SPAN)
        z1, at = room(0, 24, T)
        v1T, at = room(at, TT, D)
        hankel, at = room(at, HEADS, 384)
        q_st, at = room(at, 2, T)
        k_st, at = room(at, 2, T)
        v_st, at = room(at, 2, TT, P)
        expd, at = room(at, 4, TT, T)
        prob, at = room(at, 2, TT, T)
        probT, at = room(at, 2, 3, P)
        soft, at = room(at, 4, 4, TT)
        subk, _ = room(top - 2 * KD * T - 2 * T - 2 * PEER_HEADS * P, 2 * PEER_HEADS, P)
        qs, at = room(4 * (PICK_TURNS + 1) * T, 2, T)
        topv, at = room(at, UNITS, 2, TOPK)
        topi, at = room(at, UNITS, 2, TOPK)
        st_v, at = room(at, 2, TT, TOPK)
        st_i, at = room(at, 2, TT, TOPK)
        st_w, at = room(at, 2, TT, P)
        st_s, at = room(at, 2, TT, P)
        cand, at = room(at, UNITS, CANDS)
        cid, at = room(at, UNITS, CANDS)
        cst, at = room(at, 2, CANDS)
        cwk, at = room(at, 2, CANDS)
        pv, at = room(at, 2, TOPK)
        pi, at = room(at, 2, TOPK)
        pf, at = room(at, 2, TOPK)
        eq, at = room(at, 2, TOPK, CANDS)
        tv, at = room(at, UNITS, TOPK)
        ids, at = room(at, UNITS, TOPK)
        id_i, at = room(at, 3, UNITS * TOPK)
        id_f, at = room(at, 2, UNITS, TOPK)
        gsum, at = room(at, 2, UNITS)
        assert at <= top - 2 * KD * T - 2 * T - 2 * PEER_HEADS * P

        table = big[:].rearrange("p (i t) -> p i t", t=T)

        loaded = [sem(f"loaded{i}") for i in range(RAW)]
        hi_ready = sem("hi_ready")
        split_ready = sem("split_ready")
        half_used = sem("half_used")
        proj_taken = sem("proj_taken")
        params_in = sem("params_in")
        x_in = sem("x_in")
        subk_in = sem("subk_in")
        hankel_in = sem("hankel_in")
        line_out = sem("line_out")
        out_done = sem("out_done")
        sq_ready = [sem(f"sq_ready{i}") for i in range(5)]
        ss_ready = [sem(f"ss_ready{i}") for i in range(5)]
        rstd_step = [sem(f"rstd_step{i}") for i in range(5)]
        rstd_ready = [sem(f"rstd_ready{i}") for i in range(5)]
        h_ready = [sem(f"h_ready{i}") for i in range(7)]
        x_hi_ready = [sem(f"x_hi_ready{i}") for i in range(6)]
        operand_ready = [sem(f"operand_ready{i}") for i in range(6)]
        line_ps = sem("line_ps")
        line_sb = sem("line_sb")
        neg_row = sem("neg_row")
        gated = sem("gated")
        pad_zero = sem("pad_zero")
        pad_ready = sem("pad_ready")
        conv_step = sem("conv_step")
        tap_ready = sem("tap_ready")
        tap_used = sem("tap_used")
        conv_last = sem("conv_last")
        ln_step = [sem(f"ln_step{i}") for i in range(2)]
        ln_sum = [sem(f"ln_sum{i}") for i in range(2)]
        ln_root = [sem(f"ln_root{i}") for i in range(2)]
        silu_done = sem("silu_done")
        vn_ready = sem("vn_ready")
        vT_ps = sem("vT_ps")
        vT_ready = sem("vT_ready")
        masked = sem("masked")
        mixed = sem("mixed")
        x_added = sem("x_added")
        keys_scored = sem("keys_scored")
        rank_first = sem("rank_first")
        rank_second = sem("rank_second")
        ranked = sem("ranked")
        scores_copied = sem("scores_copied")
        pick_step = sem("pick_step")
        build_step = sem("build_step")
        soft_in = sem("soft_in")
        soft_exp = sem("soft_exp")
        picks_ps = sem("picks_ps")
        picks_ready = sem("picks_ready")
        hot_ready = sem("hot_ready")
        scattered = sem("scattered")
        act_gated = sem("act_gated")
        gates_stored = sem("gates_stored")
        late_gated = sem("late_gated")
        hot_step = sem("hot_step")
        ag_hi_ready = sem("ag_hi_ready")
        ag_ready = sem("ag_ready")
        y_added = sem("y_added")
        staged = sem("staged")
        values_staged = sem("values_staged")
        v1T_ps = sem("v1T_ps")
        v1T_ready = sem("v1T_ready")
        scores_ready = sem("scores_ready")
        soft_step = sem("soft_step")
        exp_ready = sem("exp_ready")
        divisor = sem("divisor")
        prob_ready = sem("prob_ready")
        probT_ps = sem("probT_ps")
        probT_ready = sem("probT_ready")
        heads_out = sem("heads_out")
        pair_taken = sem("pair_taken")

        SRC = dict(zip([n for n, _, _ in STREAM], [a["w_in"], a["w_out"], a["peer_q"][0], a["peer_u"][0], a["peer_v"][0],
                                                    a["w_qkv"], a["w_o"], a["peer_q"][1], a["peer_u"][1], a["peer_v"][1]]))
        scratch = nc.dram_tensor("bias_scratch", (HEADS, REL_SPAN), F32)
        scratch_ap = scratch.ap()

        def loaded_count(name, k, j):
            return 16 * (TILE0[name] // RAW + k + j // RAW + 1)

        def pairs(eng, before, first, behind):
            def body(k):
                for s in range(2):
                    m = 2 * k + s
                    past = not (isinstance(m, int) and m == 0)
                    if before and past:
                        before(m - 1, 1 - s)
                    first(m, s)
                    if behind and past:
                        behind(m - 1, 1 - s)
            sweep(eng, HEADS // 4, body, first=1)
            for step in (before, behind):
                if step:
                    step(HEADS // 2 - 1, 1)

        block = ctx.enter_context(nc.Block())

        @block.sync
        def _(sp):
            sp.dma_start(xT[:], a["xT"].rearrange("(k p) t -> p k t", p=P)).then_inc(x_in, 16)

            def load(name, src, k):
                for j in range(RAW):
                    at_least(sp, split_ready, 2 * (TILE0[name] + 4 * k + j - RAW) + 2)
                    sp.dma_start(raw[:, j, :], src[4 * k + j]).then_inc(loaded[j], 16)

            for name, tiles, _ in STREAM:
                sweep(sp, tiles // RAW, lambda k: load(name, SRC[name], k), first=1 if name == "w_in" else 0)
            o = out.rearrange("(k p) t -> p k t", p=P)
            for g in range(4):
                sp.wait_ge(h_ready[6], 2 * g + 2)
                sp.dma_start(o[:, 2 * g:2 * g + 2, :], hT[:, 2 * g:2 * g + 2, :]).then_inc(out_done, 16)
            sp.wait_ge(out_done, 64)

        @block.gpsimd
        def _(pool):
            for dst, src in ((const[:], a["const"]), (gains[:], a["gains"]), (small[:, 0:5, :], a["small"]),
                             (conv_w, a["conv_w"]), (rel[0:REL_BUCKETS, 0, :], a["rel"]),
                             (line[0:REL_BUCKETS + 1, 0, :], a["line"]),
                             (sgu_w, a["sgu_w"])):
                pool.dma_start(dst, src).then_inc(params_in, 16)
            pool.dma_start(sgu_b[0:1], a["sgu_b"]).then_inc(params_in, 16)
            pool.memset(rel[REL_BUCKETS:REL_BUCKETS + 1, 0, :], NEG).then_inc(neg_row, 1)
            pool.wait_ge(neg_row, 1)
            pool.memset(pad, 0.0).then_inc(pad_zero, 1)
            pool.wait_ge(params_in, 16 * PARAMS)
            pool.wait_ge(pad_zero, 1)
            pool.affine_select(out=sgu_wm, in_=sgu_w, compare_op=ALU.is_ge, fill=0.0, base=0,
                               pattern=[[0, SGU_HEADS], [1, P]], channel_multiplier=-1).then_inc(masked, 1)
            pool.wait_ge(line_sb, 1)
            pool.dma_start(scratch_ap, bias_line[0:HEADS, 0, :]).then_inc(line_out, 16)
            pool.wait_ge(line_out, 16)
            for layer in range(2):
                pool.dma_start(subk, a["subkeys"][layer]).then_inc(subk_in, 16)
                if layer == 0:
                    pool.wait_ge(y_added, KD)
                    pool.dma_start(hankel, bass.AP(scratch, 0, [[1, P], [REL_SPAN, HEADS], [1, 384]])).then_inc(hankel_in, 16)
                    pool.wait_ge(v1T_ready, 4)

                    def stage(k):
                        for s in range(2):
                            m = 2 * k + s
                            at_least(pool, scores_ready, 2 * (m - 2) + 2)
                            pool.tensor_copy(q_st[:, s, :], z1[:, m, :]).then_inc(staged, 1)
                            pool.tensor_copy(k_st[:, s, :], z1[:, 8 + m, :]).then_inc(staged, 1)
                            at_least(pool, heads_out, 2 * (m - 2) + 2)
                            pool.tensor_copy(v_st[:, s], v1T[:, :, bass.ds(m * P, P)]).then_inc(values_staged, 1)

                    sweep(pool, HEADS // 4, stage, first=1)

        @block.scalar
        def _(act):
            def round_half(name, k, j, b):
                u = 2 * (TILE0[name] + 4 * k + j) + b
                act.wait_ge(loaded[j % RAW], loaded_count(name, k, j))
                at_least(act, half_used, u - SPLIT + 1)
                s = (2 * j + b) % SPLIT
                act.activation(w_hi[:, s, :], raw[:, j % RAW, b * HALF:(b + 1) * HALF], ACT.Copy).then_inc(hi_ready, 1)

            def ahead(name, k, j):
                if isinstance(k, int) and TILE0[name] + 4 * k + j + 2 >= TILES:
                    return
                for b in range(2):
                    round_half(name, k, j + 2, b)

            def taking(name, take, turns, k0=0, first=0, last=0, besides=None):
                def body(k):
                    for j in range(4):
                        act.wait_ge(half_used, 2 * (TILE0[name] + 4 * (k + k0) + j) + 2)
                        take(k + k0, j)
                        ahead(name, k + k0, j)
                        if besides:
                            besides(k + k0, j)
                sweep(act, turns, body, first=first, last=last)

            def only_ahead(name, turns):
                def body(k):
                    for j in range(4):
                        ahead(name, k, j)
                sweep(act, turns, body)

            def square(r, sem_, count):
                for m in range(KD):
                    act.wait_ge(sem_, count(m))
                    act.activation(sq[:, m, :], xT[:, m, :], ACT.Square).then_inc(sq_ready[r], 1)

            def root(r):
                act.wait_ge(rstd_step[r], 2)
                act.activation(rstd[:], ms[:, 1, :], ACT.Sqrt).then_inc(rstd_ready[r], 1)

            def split_operand(s, all_at_once=False):
                for q in range(4):
                    act.wait_ge(h_ready[s], KD if all_at_once else 2 * q + 2)
                    act.activation(x_hi[:, 2 * q:2 * q + 2, :], hT[:, 2 * q:2 * q + 2, :], ACT.Copy).then_inc(x_hi_ready[s], 1)

            for j in range(2):
                for b in range(2):
                    round_half("w_in", 0, j, b)
            act.wait_ge(line_ps, 1)
            act.activation(bias_line[0:HEADS, 0, :], psum[0:HEADS, 0, :], ACT.Copy).then_inc(line_sb, 1)
            square(0, x_in, lambda m: 16)
            root(0)
            split_operand(0)
            taking("w_in", lambda k, j: act.activation(z0[:, j, k, :], proj_ps[j % 2], ACT.Copy).then_inc(proj_taken, 1), 4)
            act.wait_ge(proj_taken, PROJ0["w_out"])
            act.activation(sig, z0[:, 1], ACT.Sigmoid).then_inc(gated, 1)
            for i in (1, 0):
                act.activation(guv[:, i], z0[:, 2 + i], ACT.Gelu_apprx_tanh).then_inc(gated, 1)
            act.wait_ge(ln_step[1], 5)
            act.activation(lnstat[:, 1, 3, :], lnstat[:, 1, 2, :], ACT.Sqrt).then_inc(ln_root[1], 1)
            act.wait_ge(ln_step[1], 9)
            for c in range(KC):
                act.activation(vn[:, c, :], centred[:, 1, c, :], ACT.Identity, scale=small[:, 3, c:c + 1],
                               bias=small[:, 4, c:c + 1]).then_inc(vn_ready, 1)
            for g in range(2):
                act.wait_ge(vT_ps, g + 1)
                act.activation(vT[:, g, :], psum[:, 2 + g, :], ACT.Copy).then_inc(vT_ready, 1)
            act.wait_ge(params_in, 16 * PARAMS)

            def diagonal(tap, slot):
                at_least(act, tap_used, tap - 1)
                act.activation(taps[:, slot, :], ident, ACT.Copy, scale=conv_w[:, KC - 1, bass.ds(tap, 1)]).then_inc(tap_ready, 1)

            diagonal(0, 0)
            diagonal(1, 1)
            diagonal(2, 0)
            with act.Fori(1, CONV // 2) as k:
                diagonal(2 * k + 1, 1)
                diagonal(2 * k + 2, 0)
            act.wait_ge(tap_used, CONV)
            act.activation(conv[:, KC - 1, :], psum[:, 4, 0:T], ACT.Identity, bias=small[:, 0, KC - 1:KC]).then_inc(conv_last, 1)
            act.wait_ge(ln_step[0], 5)
            act.activation(lnstat[:, 0, 3, :], lnstat[:, 0, 2, :], ACT.Sqrt).then_inc(ln_root[0], 1)
            act.wait_ge(ln_step[0], 9)
            for c in range(KC):
                act.activation(hT[:, c, :], centred[:, 0, c, :], ACT.Silu, scale=small[:, 1, c:c + 1],
                               bias=small[:, 2, c:c + 1]).then_inc(h_ready[1], 1)
            split_operand(1, True)
            only_ahead("w_out", 2)

            def experts(l):
                act_q, act_u, act_v = f"q{l}", f"u{l}", f"v{l}"
                square(1 + 2 * l, proj_taken, lambda m: PROJ0[act_q] - KD + m + 1)
                root(1 + 2 * l)
                split_operand(2 + 3 * l)

                def take_query(k, j):
                    at_least(act, keys_scored, 16 * l + 4 * k + j - 1)
                    act.activation(qs[:, j % 2, :], proj_ps[j % 2], ACT.Copy).then_inc(proj_taken, 1)

                def take_act(k, j):
                    i = 4 * k + j
                    act.activation(big[:, bass.ds(i * T, T)], proj_ps[j % 2], ACT.Gelu_apprx_tanh).then_inc(proj_taken, 1)

                taking(act_q, take_query, 4) if l else taking_first(act_q, take_query)
                taking(act_u, take_act, PICK_TURNS)
                act.wait_ge(soft_in, l + 1)
                act.activation(tv, ids_f_tmp, ACT.Exp).then_inc(soft_exp, 1)

                def store_gates(k, j):
                    for half in range(2):
                        g = 8 * (k - PICK_TURNS) + 2 * j + half
                        act.wait_ge(scattered, 2 * GROUPS * l + g + 1)
                        act.activation(table[:, LATE:NKEYS, bass.ds(4 * g, 4)],
                                       misc_ps[half][:, 0:4 * (NKEYS - LATE)].rearrange("p (t i) -> p i t", t=4), ACT.Copy)\
                           .then_inc(gates_stored, 1)

                taking(act_u, take_act, LATE_TURN - PICK_TURNS, k0=PICK_TURNS, besides=store_gates)

                def take_fresh(k, j):
                    at_least(act, late_gated, (NKEYS - LATE) * l + 4 * (k - LATE_TURN) + j - 1)
                    act.activation(fresh[:, j % 2, :], proj_ps[j % 2], ACT.Gelu_apprx_tanh).then_inc(proj_taken, 1)

                taking(act_u, take_fresh, NKEYS // 4 - LATE_TURN, k0=LATE_TURN, first=1)

                def round_ag(k, j):
                    i = 4 * k + j + 2
                    if isinstance(i, int) and i >= NKEYS:
                        return
                    act.activation(ag_hi[:, j % 2, :], big[:, bass.ds(i * T, T)], ACT.Copy).then_inc(ag_hi_ready, 1)

                act.wait_ge(act_gated, GROUPS * (l + 1))
                act.wait_ge(late_gated, (NKEYS - LATE) * (l + 1))
                for j in range(2):
                    act.activation(ag_hi[:, j, :], big[:, j * T:(j + 1) * T], ACT.Copy).then_inc(ag_hi_ready, 1)

                def body(k):
                    for j in range(4):
                        act.wait_ge(half_used, 2 * (TILE0[act_v] + 4 * k + j) + 2)
                        round_ag(k, j)
                        ahead(act_v, k, j)
                sweep(act, NKEYS // 4, body, last=1)

            def taking_first(name, take):
                def body(k):
                    for j in range(4):
                        act.wait_ge(half_used, 2 * (TILE0[name] + 4 * k + j) + 2)
                        take(k, j)
                        ahead(name, k, j)
                sweep(act, 4, body, first=1)

            ids_f_tmp = room(top - 2 * KD * T, UNITS, TOPK)[0]
            experts(0)
            square(2, y_added, lambda m: m + 1)
            root(2)
            split_operand(3)
            taking("qkv", lambda k, j: act.activation(z1[:, bass.ds(4 * k + j, 1), :].rearrange("p a t -> p (a t)"), proj_ps[j % 2],
                                                      ACT.Copy, scale=HD ** -0.5).then_inc(proj_taken, 1), 2)
            taking("qkv", lambda k, j: act.activation(z1[:, bass.ds(4 * k + j, 1), :].rearrange("p a t -> p (a t)"), proj_ps[j % 2],
                                                      ACT.Copy).then_inc(proj_taken, 1), 4, k0=2)
            for g in range(4):
                act.wait_ge(v1T_ps, g + 1)
                act.activation(v1T[:, g // 2, 512 * (g % 2):512 * (g % 2) + 512], psum[:, g, :], ACT.Copy).then_inc(v1T_ready, 1)

            def exponentials(m, s):
                for e in range(2):
                    b = 2 * s + e
                    at_least(act, prob_ready, 2 * (m - 2) + e + 1)
                    act.wait_ge(soft_step, 4 * m + 2 * e + 2)
                    for t in range(TT):
                        act.activation(expd[:, b, t, :], psum[:, b, t * T:(t + 1) * T], ACT.Exp, bias=soft[:, b, 1, t:t + 1],
                                       accum_out=soft[:, b, 2, t:t + 1]).then_inc(exp_ready, 1)

            def turned(m, s):
                for e in range(2):
                    act.wait_ge(probT_ps, 2 * m + e + 1)
                    at_least(act, heads_out, 2 * (m - 1) + e + 1)
                    act.activation(probT[:, e].rearrange("p a b -> p (a b)"), psum[:, 4 + e, 0:3 * P], ACT.Copy).then_inc(probT_ready, 1)

            pairs(act, turned, exponentials, None)
            split_operand(4)
            only_ahead("w_o", 2)
            experts(1)
            square(4, y_added, lambda m: KD + m + 1)
            root(4)

        @block.vector
        def _(dve):
            def lower_half(name, k, j, b):
                u = 2 * (TILE0[name] + 4 * k + j) + b
                dve.wait_ge(hi_ready, u + 1)
                s = (2 * j + b) % SPLIT
                dve.tensor_tensor(w_lo[:, s, :], raw[:, j % RAW, b * HALF:(b + 1) * HALF], w_hi[:, s, :].bitcast(F32),
                                  ALU.subtract).then_inc(split_ready, 1)

            def ahead(name, k, j, last_wait=None):
                if isinstance(k, int) and TILE0[name] + 4 * k + j + 2 >= TILES:
                    return
                for b in range(2):
                    if b and last_wait:
                        dve.wait_ge(*last_wait)
                    lower_half(name, k, j + 2, b)

            def norm(r, gain, s):
                dve.wait_ge(ss_ready[r], 1)
                dve.tensor_scalar(ms[:, 0, :], misc_ps[0][:, 0:T], 1.0 / D, EPS, ALU.mult, ALU.add).then_inc(rstd_step[r], 1)
                dve.wait_ge(rstd_step[r], 1)
                dve.reciprocal(ms[:, 1, :], ms[:, 0, :]).then_inc(rstd_step[r], 1)
                dve.wait_ge(rstd_ready[r], 1)
                for m in range(KD):
                    dve.scalar_tensor_tensor(out=hT[:, m, :], in0=xT[:, m, :], scalar=gains[:, gain, m:m + 1], in1=rstd[:],
                                             op0=ALU.mult, op1=ALU.mult).then_inc(h_ready[s], 1)
                    if s < 6 and m in (4, 6):
                        lower_operand(s, m // 2 - 2)
                if s < 6:
                    lower_operand(s, 2)
                    lower_operand(s, 3)

            def lower_operand(s, q):
                dve.wait_ge(x_hi_ready[s], q + 1)
                dve.tensor_tensor(x_lo[:, 2 * q:2 * q + 2, :], hT[:, 2 * q:2 * q + 2, :],
                                  x_hi[:, 2 * q:2 * q + 2, :].bitcast(F32), ALU.subtract).then_inc(operand_ready[s], 1)

            def split_operand(s):
                for q in range(4):
                    lower_operand(s, q)

            def layer_norm(i, src):
                step, st = ln_step[i], lnstat[:, i]
                dve.wait_ge(ln_sum[i], 1)
                dve.tensor_scalar(st[:, 0, :], misc_ps[i][:, 0:T], 1.0 / CH, None, ALU.mult).then_inc(step, 1)
                dve.wait_ge(step, 1)
                dve.tensor_tensor(centred[:, i], src, st[:, 0:1, :].to_broadcast([P, KC, T]), ALU.subtract).then_inc(step, 1)
                dve.wait_ge(step, 2)
                dve.tensor_tensor(lnsq[:, i], centred[:, i], centred[:, i], ALU.mult).then_inc(step, 1)
                dve.wait_ge(ln_sum[i], 2)
                dve.tensor_scalar(st[:, 1, :], misc_ps[i][:, 0:T], 1.0 / CH, EPS, ALU.mult, ALU.add).then_inc(step, 1)
                dve.wait_ge(step, 4)
                dve.reciprocal(st[:, 2, :], st[:, 1, :]).then_inc(step, 1)
                dve.wait_ge(ln_root[i], 1)
                for c in range(KC):
                    dve.tensor_tensor(centred[:, i, c, :], centred[:, i, c, :], st[:, 3, :], ALU.mult).then_inc(step, 1)

            for j in range(2):
                for b in range(2):
                    lower_half("w_in", 0, j, b)
            dve.wait_ge(params_in, 16 * PARAMS)
            dve.wait_ge(x_in, 16)
            norm(0, 0, 0)
            sweep(dve, 4, lambda k: [ahead("w_in", k, j) for j in range(4)])
            dve.wait_ge(gated, 1)
            dve.wait_ge(pad_zero, 1)
            dve.tensor_tensor(pad[:, :, CONV - 1:CONV - 1 + T], z0[:, 0], sig, ALU.mult).then_inc(pad_ready, 1)
            layer_norm(1, guv[:, 1])
            dve.wait_ge(pad_ready, 1)
            for c in range(KC - 1):
                dve.tensor_scalar(conv[:, c, :], pad[:, c, 0:T], conv_w[:, c, 0:1], small[:, 0, c:c + 1],
                                  ALU.mult, ALU.add).then_inc(conv_step, 1)
            with dve.Fori(1, CONV) as tap:
                for c in range(KC - 1):
                    dve.wait_ge(conv_step, (KC - 1) * tap + c - KC + 2)
                    dve.scalar_tensor_tensor(out=conv[:, c, :], in0=pad[:, c, bass.ds(tap, T)], scalar=conv_w[:, c, bass.ds(tap, 1)],
                                             in1=conv[:, c, :], op0=ALU.mult, op1=ALU.add).then_inc(conv_step, 1)
            dve.wait_ge(conv_step, (KC - 1) * CONV)
            dve.wait_ge(conv_last, 1)
            layer_norm(0, conv)
            for c in range(KC):
                dve.wait_ge(mixed, c + 1)
                dve.tensor_tensor(hT[:, KC + c, :], guv[:, 0, c, :], psum[:, c // 2, (c % 2) * T:(c % 2 + 1) * T],
                                  ALU.mult).then_inc(h_ready[1], 1)
            split_operand(1)

            def add_residual(name):
                def body(k):
                    for j in range(4):
                        dve.wait_ge(half_used, 2 * (TILE0[name] + 4 * k + j) + 2)
                        x_m = xT[:, bass.ds(4 * k + j, 1), :].rearrange("p a t -> p (a t)")
                        dve.tensor_tensor(x_m, x_m, proj_ps[j % 2], ALU.add).then_inc(proj_taken, 1)
                        ahead(name, k, j)
                sweep(dve, 2, body)

            def rank_keys(l, r, s):
                n = 16 * l + r
                sti = st_i.bitcast(U32)

                def outcome(src, dst, o):
                    dst = dst.rearrange("p (t h) a r -> p t (h a) r", t=TT)
                    return dst[:, :, bass.ds(r, 1), o:o + 8], src[:, s, :, o:o + 8].rearrange("p t (a r) -> p t a r", a=1)

                def copy_scores():
                    dve.wait_ge(keys_scored, n + 1)
                    dve.tensor_copy(st_s[:, s].rearrange("p t s -> p (t s)"), misc_ps[s][:, 0:T]).then_inc(scores_copied, 1)

                def first_values():
                    for t in range(TT):
                        dve.max(st_v[:, s, t, 0:8], st_s[:, s, t, :]).then_inc(rank_first, 1)

                def first_places():
                    dve.wait_ge(rank_first, 7 * n + 2)
                    dve.tensor_copy(*outcome(st_v, topv, 0)).then_inc(rank_first, 1)
                    for t in range(TT):
                        dve.max_index(sti[:, s, t, 0:8], st_v[:, s, t, 0:8], st_s[:, s, t, :]).then_inc(rank_first, 1)
                    for t in range(TT):
                        dve.match_replace(st_w[:, s, t, :], st_v[:, s, t, 0:8], st_s[:, s, t, :], LOWEST).then_inc(rank_first, 1)

                def second_values():
                    dve.wait_ge(rank_first, 7 * n + 7)
                    dve.tensor_copy(*outcome(sti, topi, 0)).then_inc(rank_second, 1)
                    for t in range(TT):
                        dve.max(st_v[:, s, t, 8:16], st_w[:, s, t, :]).then_inc(rank_second, 1)

                def second_places():
                    dve.wait_ge(rank_second, 6 * n + 3)
                    dve.tensor_copy(*outcome(st_v, topv, 8)).then_inc(rank_second, 1)
                    for t in range(TT):
                        dve.max_index(sti[:, s, t, 8:16], st_v[:, s, t, 8:16], st_w[:, s, t, :]).then_inc(rank_second, 1)

                def places_out():
                    dve.wait_ge(rank_second, 6 * n + 6)
                    dve.tensor_copy(*outcome(sti, topi, 8)).then_inc(ranked, 1)

                return [copy_scores, first_values, first_places, second_values, second_places, places_out]

            def build_candidates(l):
                b0 = 23 * l
                dve.wait_ge(ranked, 16 * (l + 1))
                dve.wait_ge(rank_first, 7 * 16 * (l + 1))
                dve.wait_ge(rank_second, 6 * 16 * (l + 1))
                dve.tensor_scalar(topi[:, :, 0, :], topi[:, :, 0, :], float(NKEYS), None, ALU.mult).then_inc(build_step, 1)
                dve.wait_ge(build_step, b0 + 1)
                for src, dst in ((topv, cand), (topi, cid)):
                    for i0, rows, n in ROW_GROUPS:
                        o = dst[:, :, ROW_AT[i0]:ROW_AT[i0] + rows * n]
                        first, second = src[:, :, 0, i0:i0 + rows], src[:, :, 1, 0:n]
                        if rows == 1:
                            first = first.to_broadcast([P, UNITS, n])
                        elif n == 1:
                            second = second.to_broadcast([P, UNITS, rows])
                        else:
                            o = o.rearrange("p u (r n) -> p u r n", n=n)
                            first = first.rearrange("p u (r n) -> p u r n", n=1).to_broadcast([P, UNITS, rows, n])
                            second = second.rearrange("p u (r n) -> p u r n", r=1).to_broadcast([P, UNITS, rows, n])
                        dve.tensor_tensor(o, first, second, ALU.add).then_inc(build_step, 1)

            def stage_pair(k):
                dve.tensor_copy(cst, cand[:, bass.ds(2 * k, 2), :]).then_inc(pick_step, 1)

            def pick(l, k):
                s0 = 21 * (8 * l + k) + l + 1
                pos = pi.bitcast(U32)
                places = iota[:, 0:CANDS].rearrange("p (r c) -> p r c", r=1).to_broadcast([P, TOPK, CANDS])
                pair = bass.ds(2 * k, 2)

                def first_sums():
                    for e in range(2):
                        dve.max(pv[:, e, 0:8], cst[:, e, :]).then_inc(pick_step, 1)

                def first_places():
                    dve.wait_ge(pick_step, s0 + 2)
                    dve.tensor_copy(tv[:, pair, 0:8], pv[:, :, 0:8]).then_inc(pick_step, 1)
                    for e in range(2):
                        dve.max_index(pos[:, e, 0:8], pv[:, e, 0:8], cst[:, e, :]).then_inc(pick_step, 1)
                    for e in range(2):
                        dve.match_replace(cwk[:, e, :], pv[:, e, 0:8], cst[:, e, :], LOWEST).then_inc(pick_step, 1)

                def second_sums():
                    dve.wait_ge(pick_step, s0 + 7)
                    dve.tensor_copy(pf[:, :, 0:8], pos[:, :, 0:8]).then_inc(pick_step, 1)
                    for e in range(2):
                        dve.max(pv[:, e, 8:16], cwk[:, e, :]).then_inc(pick_step, 1)

                def second_places():
                    dve.wait_ge(pick_step, s0 + 10)
                    dve.tensor_copy(tv[:, pair, 8:16], pv[:, :, 8:16]).then_inc(pick_step, 1)
                    for e in range(2):
                        dve.max_index(pos[:, e, 8:16], pv[:, e, 8:16], cwk[:, e, :]).then_inc(pick_step, 1)
                    stage_pair(k if isinstance(k, int) and k == UNITS // 2 - 1 else k + 1)

                def places_out():
                    dve.wait_ge(pick_step, s0 + 13)
                    dve.tensor_copy(pf[:, :, 8:16], pos[:, :, 8:16]).then_inc(pick_step, 1)

                def compare():
                    dve.wait_ge(pick_step, s0 + 15)
                    for e in range(2):
                        dve.tensor_tensor(eq[:, e], pf[:, e, :].rearrange("p (r c) -> p r c", c=1).to_broadcast([P, TOPK, CANDS]),
                                          places, ALU.is_equal).then_inc(pick_step, 1)

                def mask_numbers():
                    for e in range(2):
                        dve.wait_ge(pick_step, s0 + 16 + e)
                        number = cid[:, bass.ds(2 * k + e, 1), :].to_broadcast([P, TOPK, CANDS])
                        dve.tensor_tensor(eq[:, e], eq[:, e], number, ALU.mult).then_inc(pick_step, 1)

                def sum_numbers():
                    for e in range(2):
                        dve.wait_ge(pick_step, s0 + 18 + e)
                        dve.tensor_reduce(ids[:, bass.ds(2 * k + e, 1), :].rearrange("p a r -> p (a r)"), eq[:, e], AX, ALU.add)\
                           .then_inc(pick_step, 1)

                return [first_sums, first_places, second_sums, second_places, places_out, compare, mask_numbers, sum_numbers]

            def finish_picks(l):
                b0 = 23 * l + 15
                diff = room(top - 2 * KD * T, UNITS, TOPK)[0]
                dve.wait_ge(pick_step, (21 * 8 + 1) * (l + 1))
                dve.tensor_tensor(diff, tv, tv[:, :, 0:1].to_broadcast([P, UNITS, TOPK]), ALU.subtract).then_inc(soft_in, 1)
                ii = id_i.bitcast(I32)
                dve.tensor_copy(ii[:, 0, :], ids.rearrange("p u r -> p (u r)")).then_inc(build_step, 1)
                dve.wait_ge(build_step, b0 + 1)
                dve.tensor_scalar(ii[:, 1, :], ii[:, 0, :], 7, None, ALU.logical_shift_right).then_inc(build_step, 1)
                dve.tensor_scalar(ii[:, 2, :], ii[:, 0, :], NKEYS - 1, None, ALU.bitwise_and).then_inc(build_step, 1)
                dve.wait_ge(build_step, b0 + 3)
                dve.tensor_copy(id_f.rearrange("p a u r -> p a (u r)"), ii[:, 1:3, :]).then_inc(build_step, 1)
                dve.wait_ge(soft_exp, l + 1)
                dve.tensor_reduce(gsum[:, 0, :], tv, AX, ALU.add).then_inc(build_step, 1)
                dve.wait_ge(build_step, b0 + 5)
                dve.reciprocal(gsum[:, 1, :], gsum[:, 0, :]).then_inc(build_step, 1)
                dve.wait_ge(build_step, b0 + 6)
                dve.tensor_tensor(tv, tv, gsum[:, 1, :].rearrange("p (u r) -> p u r", r=1).to_broadcast([P, UNITS, TOPK]),
                                  ALU.mult).then_inc(build_step, 1)
                dve.wait_ge(picks_ps, l + 1)
                dve.tensor_copy(picks[:, 0:2, :].rearrange("p a t -> p (a t)"), psum[:, 0, :]).then_inc(picks_ready, 1)
                dve.tensor_copy(picks[:, 2, :], psum[:, 1, 0:T]).then_inc(build_step, 1)
                dve.wait_ge(picks_ready, l + 1)
                dve.wait_ge(build_step, b0 + 8)

            def one_hots(l, late, g, half):
                rows = NKEYS - LATE if late else LATE
                i0 = LATE if late else 0
                r = 2 * GROUPS * l + (0 if late else GROUPS) + g
                ahead_of = [picks[:, a_, bass.ds(4 * g, 4)].rearrange("p (t i) -> p t i", i=1) for a_ in range(3)]
                numbers = iota.rearrange("p (t i) -> p t i", t=1)
                own_j, own_i = hot_j[:, 4 * half:4 * half + 4, :], hot_i[:, 4 * half:4 * half + 4, 0:rows]
                at_least(dve, scattered, r - 1)
                dve.tensor_tensor(own_i, numbers[:, :, i0:i0 + rows].to_broadcast([P, 4, rows]),
                                  ahead_of[0].to_broadcast([P, 4, rows]), ALU.is_equal).then_inc(hot_step, 1)
                dve.tensor_tensor(own_j, numbers.to_broadcast([P, 4, P]), ahead_of[1].to_broadcast([P, 4, P]),
                                  ALU.is_equal).then_inc(hot_step, 1)
                dve.wait_ge(hot_step, 2 * r + 1)
                dve.tensor_tensor(own_i, own_i, ahead_of[2].to_broadcast([P, 4, rows]), ALU.mult).then_inc(hot_ready, 1)

            def apply_gates(l, g, half):
                dve.wait_ge(scattered, 2 * GROUPS * l + GROUPS + g + 1)
                early = table[:, 0:LATE, bass.ds(4 * g, 4)]
                dve.tensor_tensor(early, early, misc_ps[half][:, 0:4 * LATE].rearrange("p (t i) -> p i t", t=4), ALU.mult)\
                   .then_inc(act_gated, 1)

            def gate_late(l, i, slot):
                dve.wait_ge(proj_taken, PROJ0[f"u{l}"] + i + 1)
                row = big[:, bass.ds(i * T, T)]
                dve.tensor_tensor(row, row, fresh[:, slot, :], ALU.mult).then_inc(late_gated, 1)

            def experts(l):
                q, u, v = f"q{l}", f"u{l}", f"v{l}"
                norm(1 + 2 * l, 2 * l + 1, 2 + 3 * l)

                def q_body(k):
                    for j in range(4):
                        if isinstance(k, int) and 4 * k + j == 0:
                            ahead(q, k, j)
                            continue
                        r = 4 * k + j - 1
                        new = rank_keys(l, r, (j - 1) % 2)
                        old = None if isinstance(r, int) and r == 0 else rank_keys(l, r - 1, j % 2)
                        new[0]()
                        lower_half(q, k, j + 2, 0)
                        if old:
                            old[3]()
                        dve.wait_ge(scores_copied, 16 * l + r + 1)
                        lower_half(q, k, j + 2, 1)
                        new[1]()
                        if old:
                            old[4]()
                        new[2]()
                        if old:
                            old[5]()

                sweep(dve, 4, q_body, first=1)
                new, old = rank_keys(l, 15, 1), rank_keys(l, 14, 0)
                new[0]()
                old[3]()
                dve.wait_ge(scores_copied, 16 * (l + 1))
                for part in (new[1], old[4], new[2], old[5], new[3], new[4], new[5]):
                    part()
                build_candidates(l)
                dve.wait_ge(build_step, 23 * l + 15)
                stage_pair(0)

                def u_body(k):
                    parts = pick(l, k)
                    for i in range(8):
                        if i == 0:
                            dve.wait_ge(pick_step, (21 * 8 + 1) * l + 21 * k + 1)
                        lower_half(u, k, i // 2 + 2, i % 2)
                        parts[i]()

                sweep(dve, PICK_TURNS - 1, u_body, first=0 if l else 1, last=1)
                for j in range(4):
                    ahead(u, PICK_TURNS - 1, j)
                finish_picks(l)

                def late_body(k):
                    for j in range(4):
                        for half in range(2):
                            one_hots(l, True, 8 * (k - PICK_TURNS) + 2 * j + half, half)
                        ahead(u, k, j)

                sweep_from(dve, PICK_TURNS, LATE_TURN, late_body, first=0 if l else 1)
                dve.wait_ge(gates_stored, GROUPS * (l + 1))
                def early_body(k):
                    for j in range(4):
                        g = 4 * (k - LATE_TURN) + j
                        one_hots(l, False, g, j % 2)
                        ahead(u, k, j)
                        if not (isinstance(g, int) and g == 0):
                            gate_late(l, LATE + g - 1, (j - 1) % 2)
                        if not (isinstance(g, int) and g < 2):
                            apply_gates(l, g - 2, j % 2)

                sweep_from(dve, LATE_TURN, NKEYS // 4, early_body, first=1)
                gate_late(l, NKEYS - 1, 1)
                for g in range(NKEYS - LATE, GROUPS + 2):
                    if g < GROUPS:
                        one_hots(l, False, g, g % 2)
                    apply_gates(l, g - 2, g % 2)

                def lower_ag(k, j):
                    i = 4 * k + j + 2
                    if isinstance(i, int) and i >= NKEYS:
                        return
                    dve.wait_ge(ag_hi_ready, NKEYS * l + i + 1)
                    dve.tensor_tensor(ag_lo[:, j % 2, :], big[:, bass.ds(i * T, T)], ag_hi[:, j % 2, :].bitcast(F32),
                                      ALU.subtract).then_inc(ag_ready, 1)

                for j in range(2):
                    lower_ag(0, j - 2)

                def v_body(k):
                    for j in range(4):
                        lower_ag(k, j)
                        ahead(v, k, j)
                sweep(dve, NKEYS // 4, v_body, last=1)
                dve.wait_ge(half_used, 2 * (TILE0[v] + NKEYS))
                for m in range(KD):
                    dve.tensor_tensor(xT[:, m, :], xT[:, m, :], y_ps[:, m, :], ALU.add).then_inc(y_added, 1)
                dve.wait_ge(y_added, KD * (l + 1))

            add_residual("w_out")
            dve.wait_ge(proj_taken, PROJ0["q0"])
            experts(0)
            norm(2, 2, 3)
            sweep(dve, 6, lambda k: [ahead("qkv", k, j) for j in range(4)])

            def maxima(m, s):
                for e in range(2):
                    b = 2 * s + e
                    dve.wait_ge(scores_ready, 2 * m + e + 1)
                    dve.tensor_reduce(soft[:, b, 0, :], psum[:, b, :].rearrange("p (t s) -> p t s", t=TT), AX, ALU.max).then_inc(soft_step, 1)
                    dve.wait_ge(soft_step, 4 * m + 2 * e + 1)
                    dve.tensor_scalar(soft[:, b, 1, :], soft[:, b, 0, :], -1.0, None, ALU.mult).then_inc(soft_step, 1)

            def probabilities(m, s):
                for e in range(2):
                    b = 2 * s + e
                    dve.wait_ge(exp_ready, 4 * m + 2 * e + 2)
                    dve.reciprocal(soft[:, b, 3, :], soft[:, b, 2, :]).then_inc(divisor, 1)
                    dve.wait_ge(divisor, 2 * m + e + 1)
                    at_least(dve, probT_ps, 2 * (m - 1) + e + 1)
                    dve.tensor_tensor(prob[:, e], expd[:, b],
                                      soft[:, b, 3, :].rearrange("p (t s) -> p t s", s=1).to_broadcast([P, TT, T]),
                                      ALU.mult).then_inc(prob_ready, 1)

            def outputs(m, s):
                dve.wait_ge(heads_out, 2 * m + 2)
                dve.tensor_copy(hT[:, bass.ds(m, 1), :].rearrange("p a t -> p (a t)"), misc_ps[s][:, 0:T]).then_inc(h_ready[4], 1)

            pairs(dve, probabilities, maxima, outputs)
            split_operand(4)
            add_residual("w_o")
            dve.wait_ge(proj_taken, PROJ0["q1"])
            experts(1)
            norm(4, 4, 6)

        @block.tensor
        def _(pe):
            def project(name, k, j, operand=None):
                n, p = TILE0[name] + 4 * k + j, PROJ0[name] + 4 * k + j
                at_least(pe, proj_taken, p - 1)
                for b in range(2):
                    pe.wait_ge(split_ready, 2 * n + b + 1)
                    s = (2 * j + b) % SPLIT
                    for i in range(4):
                        m = 4 * b + i
                        if operand is not None and isinstance(k, int) and k == j == 0 and m % 2 == 0:
                            pe.wait_ge(operand_ready[operand], m // 2 + 1)
                        hi, lo = (w[:, s, i * P:(i + 1) * P] for w in (w_hi, w_lo))
                        pe.matmul(proj_ps[j % 2], hi, x_hi[:, m, :], start=(m == 0), stop=False)
                        pe.matmul(proj_ps[j % 2], hi, x_lo[:, m, :], start=False, stop=False)
                        mm = pe.matmul(proj_ps[j % 2], lo, x_hi[:, m, :], start=False, stop=(m == KD - 1))
                    mm.then_inc(half_used, 1)

            def projections(name, tiles, operand=None):
                sweep(pe, tiles // 4, lambda k: [project(name, k, j, operand) for j in range(4)],
                      first=0 if operand is None else 1)

            def sum_squares(r):
                for m in range(KD):
                    pe.wait_ge(sq_ready[r], m + 1)
                    mm = pe.matmul(misc_ps[0][:, 0:T], ones, sq[:, m, :], start=(m == 0), stop=(m == KD - 1))
                mm.then_inc(ss_ready[r], 1)

            pe.wait_ge(params_in, 16 * PARAMS)
            pe.wait_ge(neg_row, 1)
            pe.matmul(psum[0:HEADS, 0, :], rel[0:REL_BUCKETS + 1, 0, :], line[0:REL_BUCKETS + 1, 0, :],
                      start=True, stop=True).then_inc(line_ps, 1)
            sum_squares(0)
            projections("w_in", 16, 0)

            def channel_sum(i, src):
                for c in range(KC):
                    mm = pe.matmul(misc_ps[i][:, 0:T], ones, src[:, c, :], start=(c == 0), stop=(c == KC - 1))
                mm.then_inc(ln_sum[i], 1)

            pe.wait_ge(gated, 2)
            channel_sum(1, guv[:, 1])
            pe.wait_ge(ln_step[1], 3)
            channel_sum(1, lnsq[:, 1])
            pe.wait_ge(vn_ready, KC)
            for t in range(TT):
                for c in range(KC):
                    mm = pe.transpose(psum[:, 2 + t, c * P:(c + 1) * P], vn[:, c, t * P:(t + 1) * P], ident)
                mm.then_inc(vT_ps, 1)
            pe.wait_ge(vT_ready, TT)
            pe.wait_ge(masked, 1)
            pe.wait_ge(line_sb, 1)
            for c in range(KC):
                for t in range(TT):
                    for e in range(2):
                        h = 2 * c + e
                        o = psum[HD * e:HD * (e + 1), c // 2, (c % 2) * T + t * P:(c % 2) * T + (t + 1) * P]
                        pe.matmul(o, vT[:, t, h * HD:(h + 1) * HD], sgu_wm[:, h, :], start=True, stop=False)
                        mm = pe.matmul(o, ones[0:1, 0:HD], sgu_b[0:1, h, :], start=False, stop=True)
                mm.then_inc(mixed, 1)
            pe.wait_ge(pad_ready, 1)

            def convolve(tap, slot):
                pe.wait_ge(tap_ready, tap + 1)
                pe.matmul(psum[:, 4, 0:T], taps[:, slot, :], pad[:, KC - 1, bass.ds(tap, T)],
                          start=isinstance(tap, int) and tap == 0, stop=isinstance(tap, int) and tap == CONV - 1).then_inc(tap_used, 1)

            convolve(0, 0)
            with pe.Fori(0, CONV // 2 - 1) as k:
                convolve(2 * k + 1, 1)
                convolve(2 * k + 2, 0)
            convolve(CONV - 2, 1)
            convolve(CONV - 1, 0)
            pe.wait_ge(conv_step, (KC - 1) * CONV)
            pe.wait_ge(conv_last, 1)
            channel_sum(0, conv)
            pe.wait_ge(ln_step[0], 3)
            channel_sum(0, lnsq[:, 0])
            projections("w_out", 8, 1)

            def score_keys(l, k, j):
                r = 16 * l + 4 * k + j
                pe.wait_ge(proj_taken, PROJ0[f"q{l}"] + 4 * k + j + 1)
                at_least(pe, scores_copied, r - 1)
                s = j % 2
                for t in range(TT):
                    mm = pe.matmul(misc_ps[s][:, t * P:(t + 1) * P], qs[:, s, t * P:(t + 1) * P],
                                   subk[:, bass.ds(4 * k + j, 1), :].rearrange("p a b -> p (a b)"), start=True, stop=True)
                mm.then_inc(keys_scored, 1)

            def experts(l):
                q, u, v = f"q{l}", f"u{l}", f"v{l}"
                sum_squares(1 + 2 * l)
                pe.wait_ge(subk_in, 16 * (l + 1))

                def q_body(k):
                    for j in range(4):
                        project(q, k, j, 2 + 3 * l)
                        if not (isinstance(k, int) and 4 * k + j == 0):
                            score_keys(l, k, j - 1) if j else score_keys(l, k - 1, 3)
                sweep(pe, 4, q_body, first=1)
                score_keys(l, 3, 3)
                projections(u, 4 * PICK_TURNS)
                pe.wait_ge(build_step, 23 * l + 15 + 7)
                for a_, src in enumerate((id_f[:, 0], id_f[:, 1], tv)):
                    for t in range(TT):
                        at = (a_ * TT + t) * P
                        mm = pe.transpose(psum[:, at // 512, at % 512:at % 512 + P],
                                          src.rearrange("p (t u) r -> p t (u r)", t=TT)[:, t, :], ident)
                mm.then_inc(picks_ps, 1)

                def scatter(late, g, half):
                    rows = NKEYS - LATE if late else LATE
                    r = 2 * GROUPS * l + (0 if late else GROUPS) + g
                    if late:
                        at_least(pe, gates_stored, GROUPS * l + g - 1)
                    elif isinstance(g, int) and g < 2:
                        pe.wait_ge(gates_stored, GROUPS * (l + 1))
                    else:
                        pe.wait_ge(act_gated, GROUPS * l + g - 1)
                    pe.wait_ge(hot_ready, r + 1)
                    for i in range(4):
                        mm = pe.matmul(misc_ps[half][:, i * rows:(i + 1) * rows], hot_j[:, 4 * half + i, :],
                                       hot_i[:, 4 * half + i, 0:rows], start=True, stop=True)
                    mm.then_inc(scattered, 1)

                def late_body(k):
                    for j in range(4):
                        project(u, k, j)
                        for half in range(2):
                            scatter(True, 8 * (k - PICK_TURNS) + 2 * j + half, half)

                def early_body(k):
                    for j in range(4):
                        project(u, k, j)
                        if not (isinstance(k, int) and k == LATE_TURN and j == 0):
                            scatter(False, 4 * (k - LATE_TURN) + j - 1, (j - 1) % 2)

                sweep_from(pe, PICK_TURNS, LATE_TURN, late_body, first=1)
                sweep_from(pe, LATE_TURN, NKEYS // 4, early_body, first=1)
                for g in range(NKEYS - LATE - 1, GROUPS):
                    scatter(False, g, g % 2)

                def combine(k):
                    for j in range(4):
                        n, i = TILE0[v] + 4 * k + j, 4 * k + j
                        pe.wait_ge(ag_ready, NKEYS * l + i + 1)
                        begin, end = isinstance(i, int) and i == 0, isinstance(i, int) and i == NKEYS - 1
                        for b in range(2):
                            pe.wait_ge(split_ready, 2 * n + b + 1)
                            s = (2 * j + b) % SPLIT
                            for c in range(4):
                                m = 4 * b + c
                                hi, lo = (w[:, s, c * P:(c + 1) * P] for w in (w_hi, w_lo))
                                pe.matmul(y_ps[:, m, :], hi, ag_hi[:, j % 2, :], start=begin and m % 2 == 0, stop=False, skip_group_check=True)
                                pe.matmul(y_ps[:, m, :], hi, ag_lo[:, j % 2, :], start=False, stop=False, skip_group_check=True)
                                mm = pe.matmul(y_ps[:, m, :], lo, ag_hi[:, j % 2, :], start=False, stop=end, skip_group_check=True)
                            mm.then_inc(half_used, 1)
                sweep(pe, NKEYS // 4, combine, first=1, last=1)

            experts(0)
            sum_squares(2)
            projections("qkv", 24, 3)
            pe.wait_ge(proj_taken, PROJ0["w_o"])
            for t in range(TT):
                for g in range(2):
                    for i in range(4):
                        mm = pe.transpose(psum[:, 2 * t + g, i * P:(i + 1) * P], z1[:, 16 + 4 * g + i, t * P:(t + 1) * P], ident)
                    mm.then_inc(v1T_ps, 1)
            pe.wait_ge(v1T_ready, 4)
            pe.wait_ge(hankel_in, 16)

            def scores(m, s):
                pe.wait_ge(staged, 2 * m + 2)
                for e in range(2):
                    h = 2 * m + e
                    at_least(pe, exp_ready, 4 * (m - 2) + 2 * e + 2)
                    for t in range(TT):
                        o = psum[:, 2 * s + e, t * T:(t + 1) * T]
                        pe.matmul(o, anti, hankel[:, bass.ds(h, 1), (TT - 1 - t) * P:(TT - 1 - t) * P + T].rearrange("p a t -> p (a t)"),
                                  start=True, stop=False, skip_group_check=True)
                        mm = pe.matmul(o[:, 0:(t + 1) * P], q_st[HD * e:HD * (e + 1), s, t * P:(t + 1) * P],
                                       k_st[HD * e:HD * (e + 1), s, 0:(t + 1) * P], start=False, stop=True, skip_group_check=True)
                    mm.then_inc(scores_ready, 1)

            def outcomes(m, s):
                for e in range(2):
                    pe.wait_ge(prob_ready, 2 * m + e + 1)
                    at_least(pe, probT_ready, 2 * (m - 1) + e + 1)
                    for i, (t, c) in enumerate(((0, 0), (1, 0), (1, 1))):
                        mm = pe.transpose(psum[:, 4 + e, i * P:(i + 1) * P], prob[:, e, t, c * P:(c + 1) * P], ident)
                    mm.then_inc(probT_ps, 1)
                at_least(pe, h_ready[4], m - 1)
                pe.wait_ge(values_staged, m + 1)
                for e in range(2):
                    pe.wait_ge(probT_ready, 2 * m + e + 1)
                    o = misc_ps[s][HD * e:HD * (e + 1), 0:T]
                    pe.matmul(o, v_st[:, s, 0, HD * e:HD * (e + 1)], probT[:, e, 0:2, :].rearrange("p a b -> p (a b)"),
                              start=True, stop=False, skip_group_check=True)
                    pe.matmul(o[:, P:T], v_st[:, s, 1, HD * e:HD * (e + 1)], probT[:, e, 2, :],
                              start=False, stop=True, skip_group_check=True).then_inc(heads_out, 1)

            pairs(pe, None, scores, outcomes)
            projections("w_o", 8, 4)
            experts(1)
            sum_squares(4)


def kernel(x, ev_w_in, ev_conv_w, ev_conv_b, ev_conv_ln_g, ev_conv_ln_b, ev_sgu_ln_g, ev_sgu_ln_b, ev_sgu_w, ev_sgu_b,
           ev_w_out, od_w_qkv, od_w_o, rel_bias, peer_w_q, peer_subkeys, peer_u, peer_v,
           norm_mix_g, norm_ffn_g, norm_final_g):
    import concourse.bacc as bacc
    from concourse.bass_utils import run_bass_kernel_spmd

    f = np.asarray

    def tiles(w):
        return np.ascontiguousarray(f(w).reshape(KD, P, -1, P).transpose(2, 1, 0, 3)).reshape(-1, P, D)

    def columns(v, n):
        return np.ascontiguousarray(f(v).reshape(n, P).T)

    w_in = tiles(ev_w_in[0])
    w_in = np.ascontiguousarray(w_in.reshape(4, KC, P, D).transpose(1, 0, 2, 3)).reshape(-1, P, D)
    const, line = constants()
    gains = np.stack([columns(g, KD) for g in (norm_mix_g[0], norm_ffn_g[0], norm_mix_g[1], norm_ffn_g[1], norm_final_g)], 1)
    small = np.stack([columns(g[0], KC) for g in (ev_conv_b, ev_conv_ln_g, ev_conv_ln_b, ev_sgu_ln_g, ev_sgu_ln_b)], 1)
    arrays = {
        "xT": np.ascontiguousarray(f(x)[0].T),
        "w_in": w_in, "w_out": tiles(ev_w_out[0]), "w_qkv": tiles(od_w_qkv[0]), "w_o": tiles(od_w_o[0]),
        "peer_q0": tiles(peer_w_q[0]), "peer_q1": tiles(peer_w_q[1]),
        "peer_u0": tiles(f(peer_u[0]).T), "peer_u1": tiles(f(peer_u[1]).T),
        "peer_v0": f(peer_v[0]).reshape(NKEYS, P, D), "peer_v1": f(peer_v[1]).reshape(NKEYS, P, D),
        "subkeys": np.ascontiguousarray(f(peer_subkeys).reshape(2, 2 * PEER_HEADS, NKEYS, P).transpose(0, 3, 1, 2)),
        "const": const, "line": line, "gains": gains, "small": small,
        "conv_w": np.ascontiguousarray(f(ev_conv_w[0]).reshape(CONV, KC, P).transpose(2, 1, 0)),
        "rel": f(rel_bias),
        "sgu_w": np.ascontiguousarray(f(ev_sgu_w[0]).transpose(2, 0, 1)),
        "sgu_b": f(ev_sgu_b[0]).reshape(1, SGU_HEADS, P),
    }
    nc = bacc.Bacc("TRN2", target_bir_lowering=False, num_devices=1)
    arrays = {f"in_{n}": v for n, v in arrays.items()}
    given = {n[3:]: nc.dram_tensor(n, v.shape, F32, kind="ExternalInput").ap() for n, v in arrays.items()}
    out = nc.dram_tensor("out", (D, T), F32, kind="ExternalOutput").ap()
    for n in ("peer_q", "peer_u", "peer_v"):
        given[n] = [given[f"{n}{l}"] for l in range(2)]
    build(nc, given, out)
    r = run_bass_kernel_spmd(nc, [arrays], core_ids=[0])
    return np.ascontiguousarray(r.results[0]["out"].T).reshape(1, T, D)
```
